# Optimizing a Trainium2 kernel written in Bass

```python
import math
import jax, jax.numpy as jnp
from jax import lax
import numpy as np

D_MODEL = 1024
BATCH = 1
SEQ = 128
DEPTH = 2
DEC_BATCH = 1
DEC_SEQ = 1024
PAST_LEN = 256

GRID_W = 64
HEAD_DIM = 64
ROPE_FREQS = HEAD_DIM // 4
ROPE_THETA = 10000.0
Q_BLOCK = 128
EPS = 1e-6
A_HEADS = D_MODEL // (2 * HEAD_DIM)
A_KV_HEADS = A_HEADS // 4
A_Q_W = A_HEADS * HEAD_DIM
A_KV_W = A_KV_HEADS * HEAD_DIM
LRU_WIDTH = D_MODEL // 2
LRU_BLOCKS = 8
LRU_BLOCK_W = LRU_WIDTH // LRU_BLOCKS
CONV_W = 4
CONV_LEFT = 1
RG_C = 8.0
HYB_SPLITS = (A_Q_W, A_Q_W + A_KV_W, A_Q_W + 2 * A_KV_W, A_Q_W + 2 * A_KV_W + LRU_WIDTH)
HYB_IN_W = A_Q_W + 2 * A_KV_W + 2 * LRU_WIDTH
C_HEADS = D_MODEL // (2 * HEAD_DIM)
C_IN_W = 3 * 2 * C_HEADS * HEAD_DIM
N_EXPERTS = 16
EXPERT_FF = D_MODEL
EC_FACTOR = 2
ADA_CHUNKS = 6

kernel_name = 'hybrid_diffusion_prefix_trunk_step'

def rms_norm(x, g):
    xf = x.astype(jnp.float32)
    y = xf * lax.rsqrt(jnp.mean(xf * xf, axis=-1, keepdims=True) + EPS)
    return (y * g.astype(jnp.float32)).astype(x.dtype)

def adaln(cond, w, b):
    m = jax.nn.silu(cond) @ w + b
    return [t[:, None, :] for t in jnp.split(m, ADA_CHUNKS, axis=-1)]

def modulate(h, shift, scale):
    return h * (1 + scale) + shift

def axial_rope_tables(n_tokens):
    rows = n_tokens // GRID_W
    pos_r = jnp.repeat(jnp.arange(rows, dtype=jnp.float32), GRID_W)
    pos_c = jnp.tile(jnp.arange(GRID_W, dtype=jnp.float32), rows)
    inv = ROPE_THETA ** (-jnp.arange(ROPE_FREQS, dtype=jnp.float32) / ROPE_FREQS)
    ang = jnp.stack([pos_r[:, None] * inv, pos_c[:, None] * inv], axis=1)
    return jnp.cos(ang), jnp.sin(ang)

def apply_axial_rope(x, cos, sin):
    L = x.shape[1]
    bshape = (1, L) + (1,) * (x.ndim - 3) + (2, ROPE_FREQS)
    cs = cos.reshape(bshape).astype(x.dtype)
    sn = sin.reshape(bshape).astype(x.dtype)
    xr = x.reshape(x.shape[:-1] + (2, 2, ROPE_FREQS))
    x1, x2 = xr[..., 0, :], xr[..., 1, :]
    out = jnp.stack([x1 * cs - x2 * sn, x2 * cs + x1 * sn], axis=-2)
    return out.reshape(x.shape)

def blocked_gqa(q, k, v):
    B, Lq, H, D = q.shape
    kvh = k.shape[2]
    grp = H // kvh
    nb = Lq // Q_BLOCK
    qb = q.reshape(B, nb, Q_BLOCK, kvh, grp, D).transpose(1, 0, 2, 3, 4, 5)
    scale = D ** -0.5

    def one_block(qblk):
        s = jnp.einsum('bqkgd,bskd->bkgqs', qblk, k, preferred_element_type=jnp.float32) * scale
        pr = jax.nn.softmax(s, axis=-1).astype(v.dtype)
        return jnp.einsum('bkgqs,bskd->bqkgd', pr, v)

    o = lax.map(one_block, qb)
    return o.transpose(1, 0, 2, 3, 4, 5).reshape(B, Lq, H * D)

def blocked_diff_attention(q, k, v, lam):
    B, Lq, _, H, D = q.shape
    nb = Lq // Q_BLOCK
    qb = q.reshape(B, nb, Q_BLOCK, 2, H, D).transpose(1, 0, 2, 3, 4, 5)
    scale = D ** -0.5

    def one_block(qblk):
        s = jnp.einsum('bqphd,bsphd->bphqs', qblk, k, preferred_element_type=jnp.float32) * scale
        pr = jax.nn.softmax(s, axis=-1)
        w = (pr[:, 0] - lam * pr[:, 1]).astype(v.dtype)
        return jnp.einsum('bhqs,bshe->bqhe', w, v)

    o = lax.map(one_block, qb)
    return o.transpose(1, 0, 2, 3, 4).reshape(B, Lq, H, 2 * D)

def centred_dwconv(x, w, b):
    L = x.shape[1]
    xp = jnp.pad(x, ((0, 0), (CONV_LEFT, CONV_W - 1 - CONV_LEFT), (0, 0)))
    return b + sum(xp[:, j:j + L] * w[j] for j in range(CONV_W))

def _lin_combine(e1, e2):
    a1, b1 = e1
    a2, b2 = e2
    return a1 * a2, a2 * b1 + b2

def rglru_scan(x, prm, h0, reverse):
    wa, ba, wi, bi, lam = prm
    B, L, W = x.shape
    f32 = jnp.float32
    xf = x.astype(f32)
    xblk = xf.reshape(B, L, LRU_BLOCKS, LRU_BLOCK_W)
    r = jax.nn.sigmoid(jnp.einsum('blnd,nde->blne', xblk, wa.astype(f32)).reshape(B, L, W) + ba.astype(f32))
    i = jax.nn.sigmoid(jnp.einsum('blnd,nde->blne', xblk, wi.astype(f32)).reshape(B, L, W) + bi.astype(f32))
    log_a = -RG_C * r * jax.nn.softplus(-lam.astype(f32))
    a = jnp.exp(log_a)
    b = jnp.sqrt(-jnp.expm1(2.0 * log_a)) * (i * xf)
    if reverse:
        a, b = jnp.flip(a, axis=1), jnp.flip(b, axis=1)
    acc_a, acc_b = lax.associative_scan(_lin_combine, (a, b), axis=1)
    hs = acc_a * h0.astype(f32)[:, None, :] + acc_b
    if reverse:
        hs = jnp.flip(hs, axis=1)
    return hs

def hybrid_mixer(h, p, ctx, rope):
    B, L, _ = h.shape
    q, k, v, xb, gb = jnp.split(h @ p['w_in'], HYB_SPLITS, axis=-1)
    q = rms_norm(q.reshape(B, L, A_HEADS, HEAD_DIM), p['q_gain'])
    k = rms_norm(k.reshape(B, L, A_KV_HEADS, HEAD_DIM), p['k_gain'])
    v = v.reshape(B, L, A_KV_HEADS, HEAD_DIM)
    xc = centred_dwconv(xb, p['conv_w'], p['conv_b'])
    if ctx is None:
        kk, vv = k, v
        h0f = jnp.zeros((B, LRU_WIDTH), jnp.float32)
        h0b = h0f
    else:
        ck, cv, h0f, h0b = ctx
        q = apply_axial_rope(q, *rope)
        k = apply_axial_rope(k, *rope)
        kk = jnp.concatenate([ck, k], axis=1)
        vv = jnp.concatenate([cv, v], axis=1)
    attn = blocked_gqa(q, kk, vv)
    hf = rglru_scan(xc, p['fwd'], h0f, reverse=False)
    hb = rglru_scan(xc, p['bwd'], h0b, reverse=True)
    rec = (hf + hb).astype(h.dtype) * jax.nn.gelu(gb)
    out = jnp.concatenate([attn, rec], axis=-1) @ p['w_out']
    if ctx is None:
        state = (k, v, hf[:, -1].astype(h.dtype), hb[:, 0].astype(h.dtype))
    else:
        state = None
    return out, state

def diff_mixer(h, p, ctx, rope):
    B, L, _ = h.shape
    f32 = jnp.float32
    q, k, v = jnp.split(h @ p['w_in'], 3, axis=-1)
    q = rms_norm(q.reshape(B, L, 2, C_HEADS, HEAD_DIM), p['q_gain'])
    k = rms_norm(k.reshape(B, L, 2, C_HEADS, HEAD_DIM), p['k_gain'])
    v = v.reshape(B, L, C_HEADS, 2 * HEAD_DIM)
    lam = (jnp.exp(jnp.sum(p['lam_q1'].astype(f32) * p['lam_k1'].astype(f32)))
           - jnp.exp(jnp.sum(p['lam_q2'].astype(f32) * p['lam_k2'].astype(f32)))
           + p['lam_init'])
    if ctx is None:
        kk, vv = k, v
        state = (k, v)
    else:
        ck, cv = ctx
        q = apply_axial_rope(q, *rope)
        k = apply_axial_rope(k, *rope)
        kk = jnp.concatenate([ck, k], axis=1)
        vv = jnp.concatenate([cv, v], axis=1)
        state = None
    o = blocked_diff_attention(q, kk, vv, lam)
    o = rms_norm(o, p['subln']) * (1.0 - p['lam_init'])
    return o.reshape(B, L, C_HEADS * 2 * HEAD_DIM) @ p['w_out'], state

def ec_moe(h, p):
    B, L, D = h.shape
    n = B * L
    cap = EC_FACTOR * n // N_EXPERTS
    xt = h.reshape(n, D)
    aff = jax.nn.softmax(jnp.matmul(xt, p['router'], preferred_element_type=jnp.float32), axis=-1)
    gate, idx = lax.top_k(aff.T, cap)
    xe = jnp.take(xt, idx, axis=0)
    hid = jax.nn.silu(jnp.einsum('ecd,edf->ecf', xe, p['w_gate'])) * jnp.einsum('ecd,edf->ecf', xe, p['w_up'])
    ye = jnp.einsum('ecf,efd->ecd', hid, p['w_down']) * gate[..., None].astype(h.dtype)
    out = jnp.zeros_like(xt).at[idx.reshape(-1)].add(ye.reshape(-1, D))
    return out.reshape(B, L, D)

def trunk_layer(x, cond, p, mixer, ctx, rope):
    sh1, sc1, g1, sh2, sc2, g2 = adaln(cond, p['ada_w'], p['ada_b'])
    mix, state = mixer(modulate(rms_norm(x, p['norm1']), sh1, sc1), p, ctx, rope)
    x = x + g1 * mix
    x = x + g2 * ec_moe(modulate(rms_norm(x, p['norm2']), sh2, sc2), p)
    return x, state

def diff_lambda_init(layer_idx):
    return 0.8 - 0.6 * math.exp(-0.3 * layer_idx)

def setup_inputs(seed: int = 0) -> dict:
    key = jax.random.key(seed)
    keys = jax.random.split(key, 128)
    ctr = [0]

    def nk():
        ctr[0] += 1
        return keys[ctr[0]]

    def nrm(shape, scale=1.0):
        return jax.random.normal(nk(), shape, jnp.float32) * scale

    def gain(n):
        return 1.0 + nrm((n,), 0.02)

    def lru_lambda():
        u = jax.random.uniform(nk(), (LRU_WIDTH,), jnp.float32, 0.9, 0.999)
        a0 = u ** (1.0 / RG_C)
        return jnp.log(a0) - jnp.log1p(-a0)

    d = D_MODEL
    inp = {}
    inp['x_prompt'] = nrm((BATCH, SEQ, d))
    inp['x_sample'] = nrm((DEC_BATCH, DEC_SEQ, d))
    inp['cache_l0_k'] = nrm((DEC_BATCH, PAST_LEN, A_KV_HEADS, HEAD_DIM))
    inp['cache_l0_v'] = nrm((DEC_BATCH, PAST_LEN, A_KV_HEADS, HEAD_DIM))
    inp['state_l0_fwd'] = nrm((DEC_BATCH, LRU_WIDTH), 0.5)
    inp['state_l0_bwd'] = nrm((DEC_BATCH, LRU_WIDTH), 0.5)
    inp['cache_l1_k'] = nrm((DEC_BATCH, PAST_LEN, 2, C_HEADS, HEAD_DIM))
    inp['cache_l1_v'] = nrm((DEC_BATCH, PAST_LEN, C_HEADS, 2 * HEAD_DIM))
    inp['c'] = nrm((DEC_BATCH, d))
    inp['c_ctx'] = nrm((d,))
    for l in range(DEPTH):
        pre = 'l%d_' % l
        inp[pre + 'norm1'] = gain(d)
        inp[pre + 'norm2'] = gain(d)
        inp[pre + 'ada_w'] = nrm((d, ADA_CHUNKS * d), 0.5 * d ** -0.5)
        inp[pre + 'ada_b'] = nrm((ADA_CHUNKS * d,), 0.02)
        if l % 2 == 0:
            inp[pre + 'w_in'] = nrm((d, HYB_IN_W), d ** -0.5)
            inp[pre + 'q_gain'] = gain(HEAD_DIM)
            inp[pre + 'k_gain'] = gain(HEAD_DIM)
            inp[pre + 'conv_w'] = nrm((CONV_W, LRU_WIDTH), CONV_W ** -0.5)
            inp[pre + 'conv_b'] = nrm((LRU_WIDTH,), 0.01)
            for dr in ('fwd', 'bwd'):
                inp[pre + dr + '_wa'] = nrm((LRU_BLOCKS, LRU_BLOCK_W, LRU_BLOCK_W), LRU_BLOCK_W ** -0.5)
                inp[pre + dr + '_ba'] = nrm((LRU_WIDTH,), 0.01)
                inp[pre + dr + '_wi'] = nrm((LRU_BLOCKS, LRU_BLOCK_W, LRU_BLOCK_W), LRU_BLOCK_W ** -0.5)
                inp[pre + dr + '_bi'] = nrm((LRU_WIDTH,), 0.01)
                inp[pre + dr + '_lam'] = lru_lambda()
            inp[pre + 'w_out'] = nrm((A_Q_W + LRU_WIDTH, d), (A_Q_W + LRU_WIDTH) ** -0.5)
        else:
            inp[pre + 'w_in'] = nrm((d, C_IN_W), d ** -0.5)
            inp[pre + 'q_gain'] = gain(HEAD_DIM)
            inp[pre + 'k_gain'] = gain(HEAD_DIM)
            inp[pre + 'lam_q1'] = nrm((HEAD_DIM,), 0.1)
            inp[pre + 'lam_k1'] = nrm((HEAD_DIM,), 0.1)
            inp[pre + 'lam_q2'] = nrm((HEAD_DIM,), 0.1)
            inp[pre + 'lam_k2'] = nrm((HEAD_DIM,), 0.1)
            inp[pre + 'subln'] = gain(2 * HEAD_DIM)
            inp[pre + 'w_out'] = nrm((2 * C_HEADS * HEAD_DIM, d), (2 * C_HEADS * HEAD_DIM) ** -0.5)
        inp[pre + 'router'] = nrm((d, N_EXPERTS), d ** -0.5)
        inp[pre + 'w_gate'] = nrm((N_EXPERTS, d, EXPERT_FF), d ** -0.5)
        inp[pre + 'w_up'] = nrm((N_EXPERTS, d, EXPERT_FF), d ** -0.5)
        inp[pre + 'w_down'] = nrm((N_EXPERTS, EXPERT_FF, d), EXPERT_FF ** -0.5)
    return inp

def reference(x_prompt, x_sample, cache_l0_k, cache_l0_v, state_l0_fwd, state_l0_bwd,
              cache_l1_k, cache_l1_v, c, c_ctx,
              l0_norm1, l0_norm2, l0_ada_w, l0_ada_b, l0_w_in, l0_q_gain, l0_k_gain,
              l0_conv_w, l0_conv_b,
              l0_fwd_wa, l0_fwd_ba, l0_fwd_wi, l0_fwd_bi, l0_fwd_lam,
              l0_bwd_wa, l0_bwd_ba, l0_bwd_wi, l0_bwd_bi, l0_bwd_lam,
              l0_w_out, l0_router, l0_w_gate, l0_w_up, l0_w_down,
              l1_norm1, l1_norm2, l1_ada_w, l1_ada_b, l1_w_in, l1_q_gain, l1_k_gain,
              l1_lam_q1, l1_lam_k1, l1_lam_q2, l1_lam_k2, l1_subln, l1_w_out,
              l1_router, l1_w_gate, l1_w_up, l1_w_down):
    layers = (
        dict(norm1=l0_norm1, norm2=l0_norm2, ada_w=l0_ada_w, ada_b=l0_ada_b,
             w_in=l0_w_in, q_gain=l0_q_gain, k_gain=l0_k_gain,
             conv_w=l0_conv_w, conv_b=l0_conv_b,
             fwd=(l0_fwd_wa, l0_fwd_ba, l0_fwd_wi, l0_fwd_bi, l0_fwd_lam),
             bwd=(l0_bwd_wa, l0_bwd_ba, l0_bwd_wi, l0_bwd_bi, l0_bwd_lam),
             w_out=l0_w_out, router=l0_router, w_gate=l0_w_gate, w_up=l0_w_up, w_down=l0_w_down),
        dict(norm1=l1_norm1, norm2=l1_norm2, ada_w=l1_ada_w, ada_b=l1_ada_b,
             w_in=l1_w_in, q_gain=l1_q_gain, k_gain=l1_k_gain,
             lam_q1=l1_lam_q1, lam_k1=l1_lam_k1, lam_q2=l1_lam_q2, lam_k2=l1_lam_k2,
             lam_init=diff_lambda_init(1), subln=l1_subln,
             w_out=l1_w_out, router=l1_router, w_gate=l1_w_gate, w_up=l1_w_up, w_down=l1_w_down),
    )
    caches = ((cache_l0_k, cache_l0_v, state_l0_fwd, state_l0_bwd), (cache_l1_k, cache_l1_v))
    mixers = (hybrid_mixer, diff_mixer)
    ctx_cond = c_ctx[None, :]
    rope = axial_rope_tables(x_sample.shape[1])
    y_p, y_s = x_prompt, x_sample
    new_state = []
    for layer in range(DEPTH):
        p = layers[layer]
        mixer = mixers[layer % 2]
        y_p, st = trunk_layer(y_p, ctx_cond, p, mixer, None, None)
        y_s, _ = trunk_layer(y_s, c, p, mixer, caches[layer], rope)
        new_state.append(st)
    (k0, v0, hf0, hb0), (k1, v1) = new_state
    return (y_p, y_s, k0, v0, hf0, hb0, k1, v1)


_drawn_inputs = setup_inputs


def setup_inputs(seed=0):
    import zlib

    import numpy as np

    out = dict(_drawn_inputs(seed))
    spreads = {}
    factors = {'cache_l0_k': 8.0,
     'cache_l0_v': 8.0,
     'state_l0_fwd': 3.496,
     'state_l0_bwd': 3.378,
     'l0_norm1': 2.901,
     'l0_norm2': 8.0,
     'l0_q_gain': 8.0,
     'l0_k_gain': 2.851,
     'l0_fwd_ba': 8.0,
     'l0_fwd_bi': 8.0,
     'l0_bwd_ba': 8.0,
     'l0_bwd_bi': 8.0,
     'l1_norm1': 3.012,
     'l1_norm2': 7.0,
     'l1_q_gain': 8.0,
     'l1_k_gain': 3.697,
     'l1_lam_k1': 32.117,
     'l1_lam_q2': 20.899,
     'l1_lam_k2': 34.05,
     'l1_subln': 39.451}
    for name, (base, spread) in spreads.items():
        noise = np.random.default_rng([zlib.crc32(name.encode()), seed]).standard_normal(out[name].shape)
        drawn = base * np.exp(spread * noise) if base else spread * noise
        out[name] = __import__('jax').numpy.asarray(drawn.astype(out[name].dtype))
    for name, factor in factors.items():
        out[name] = (out[name] * factor).astype(out[name].dtype)
    return out
```

```python
from contextlib import ExitStack

import numpy as np

import concourse.bass as bass
from concourse import mybir

F32 = mybir.dt.float32
F32R = mybir.dt.float32r
U32 = mybir.dt.uint32
I32 = mybir.dt.int32
ALU = mybir.AluOpType
ACT = mybir.ActivationFunctionType
AX = mybir.AxisListType
ds = bass.ds

P = 128
D = 1024
KB = D // P
LAT, CTX = 1024, 128
TOK = LAT + CTX
LT = LAT // P
NT = TOK // P
PAST = 256
PT_TILES = PAST // P
KEYS = PAST + LAT
KT = KEYS // P
HD = 64
EPS = 1e-6
LRU = 512
LC = LRU // P
EXP = 16
CAP_L, CAP_C = 2 * LAT // EXP, 2 * CTX // EXP
ROWS = CAP_L + CAP_C
BANK = 512
LAM_INIT = 0.8 - 0.6 * float(np.exp(-0.3))
GELU_C = float(np.sqrt(2.0 / np.pi))

VEC_A = dict(l0_norm1=0, l0_norm2=8, l1_norm1=16, l1_norm2=24, l0_ada_b=32, l1_ada_b=80)
VEC_B = dict(conv_w=0, conv_b=16, l0_fwd_ba=20, l0_fwd_bi=24, l0_bwd_ba=28, l0_bwd_bi=32,
             l0_fwd_lam=36, l0_bwd_lam=40, state_l0_fwd=44, state_l0_bwd=48, c=52, c_ctx=60, subln=68)
VEC_B_ROWS = 69


class Memory:
    pass


def wait_value(m, eng, sem, value):
    eng.wait_ge(sem, value)
    eng.sem_inc(m.passed[eng.engine], 1)


def memory(nc, ctx):
    m = Memory()
    base = (nc.sbuf_base + 63) // 64 * 64
    region = KB * TOK * 4
    region_at = [base, base + region]

    def tensor(name, shape, dt, offset):
        return nc.alloc_sbuf_tensor_at(name, shape, dt, offset=offset)

    m.region = [tensor(f"region{i}", [P, KB, TOK], F32, region_at[i]) for i in range(2)]
    m.region_at = region_at
    pos = [base + 2 * region]

    def keep(name, shape, dt=F32):
        t = tensor(name, shape, dt, pos[0])
        pos[0] += (int(np.prod(shape[1:])) * 4 + 31) // 32 * 32
        return t

    m.ident = keep("ident", [P, P])
    m.ones = keep("ones", [P, 8])
    m.neg_half = keep("neg_half", [P, 32])
    m.vec_a = keep("vec_a", [P, P])
    m.vec_b = keep("vec_b", [P, P])
    m.cond = keep("cond", [P, 2, KB])
    m.mod = [keep(f"mod{l}", [P, 48, 2]) for l in range(2)]
    m.norm_scale = [[keep(f"norm_scale{l}{i}", [P, KB, 2]) for i in range(2)] for l in range(2)]
    m.ssq = keep("ssq", [P, 32])
    m.rstd = keep("rstd", [P, 32])
    m.gate_bias = keep("gate_bias", [P, 16])
    m.decay = keep("decay", [P, 3, 8])
    m.neg_lambda = keep("neg_lambda", [P, 8])
    m.subln = keep("subln_col", [P, 8])
    m.scratch_at = pos[0]
    m.lam_rows = tensor("lam_rows", [P, 4, HD], F32, pos[0] + 6 * 16384)
    m.tensor = tensor
    m.end = nc.sbuf_usable_end
    m.psum = ctx.enter_context(nc.psum_tensor("psum", [P, 8 * BANK], F32))
    return m


def placer(m, prefix, start, end):
    pos = [start]

    def put(name, shape, dt=F32):
        size = (int(np.prod(shape[1:])) * 4 + 31) // 32 * 32
        t = m.tensor(f"{prefix}_{name}", shape, dt, pos[0])
        pos[0] += size
        assert pos[0] <= end, (prefix, name, pos[0] - end)
        return t

    put.pos = pos
    return put


def setup(nc, m, a, sem, ada_ahead):
    xin = m.region[1]
    xin_tok = xin[:, :, :].rearrange("p k t -> p (k t)").rearrange("p (t d) -> p t d", d=D)
    x = m.region[0]
    put = placer(m, "setup", m.scratch_at + 5 * 16384, m.end)
    rows = put("rows", [P, 2, P])
    lam_rows = m.lam_rows
    x_loaded = [sem(f"x_loaded{t}") for t in range(NT)]
    rows_loaded, rows_zeroed = sem("rows_loaded"), sem("rows_zeroed")
    ident_ready, turned = sem("ident_ready"), sem("turned")
    read_act, read_dve = sem("read_act"), sem("read_dve")
    vec_turned, vec_ready, silu_done = (sem(n) for n in ("vec_turned", "vec_ready", "silu_done"))
    small = [(a["l0_norm1"], 0, 0, 8), (a["l0_norm2"], 0, 8, 8), (a["l1_norm1"], 0, 16, 8), (a["l1_norm2"], 0, 24, 8),
             (a["l0_ada_b"], 0, 32, 48), (a["l1_ada_b"], 0, 80, 48),
             (a["l0_conv_w"].rearrange("j n -> (j n)"), 1, 0, 16)]
    small += [(v, 1, VEC_B[n], r) for n, v, r in (
        ("conv_b", a["l0_conv_b"], 4), ("l0_fwd_ba", a["l0_fwd_ba"], 4), ("l0_fwd_bi", a["l0_fwd_bi"], 4),
        ("l0_bwd_ba", a["l0_bwd_ba"], 4), ("l0_bwd_bi", a["l0_bwd_bi"], 4), ("l0_fwd_lam", a["l0_fwd_lam"], 4),
        ("l0_bwd_lam", a["l0_bwd_lam"], 4), ("state_l0_fwd", a["state_l0_fwd"].rearrange("b n -> (b n)"), 4),
        ("state_l0_bwd", a["state_l0_bwd"].rearrange("b n -> (b n)"), 4),
        ("c", a["c"].rearrange("b n -> (b n)"), 8), ("c_ctx", a["c_ctx"], 8), ("subln", a["l1_subln"], 1))]
    lams = [a["l1_lam_q1"], a["l1_lam_k1"], a["l1_lam_q2"], a["l1_lam_k2"]]
    n_small = len(small) + len(lams)
    batches = [(t, h) for t in range(NT) for h in range(2)]

    with nc.Block() as block:
        @block.sync
        def _(sp):
            for t in range(NT):
                src = a["x_sample"][0, t * P:(t + 1) * P, :] if t < LT else a["x_prompt"][0]
                sp.dma_start(xin_tok[:, t, :], src).then_inc(x_loaded[t], 16)
            sp.wait_ge(x_loaded[NT - 1], 16)
            sp.wait_ge(rows_loaded, 16 * n_small)
            ada_ahead(sp)

        @block.scalar
        def _(act):
            act.wait_ge(rows_zeroed, 1)
            for v, which, at, n in small:
                act.dma_start(rows[at:at + n, which, :], v.rearrange("(n p) -> n p", p=P)).then_inc(rows_loaded, 16)
            for i, v in enumerate(lams):
                act.dma_start(lam_rows[:, i, :], v.unsqueeze(0).broadcast_to([P, HD])).then_inc(rows_loaded, 16)
            for i, (t, h) in enumerate(batches):
                if i % 2 == 0:
                    act.wait_ge(turned, i + 1)
                    act.copy(x[:, 4 * h:4 * h + 4, t * P:(t + 1) * P],
                             m.psum[:, (i % 4) * BANK:(i % 4 + 1) * BANK].rearrange("p (k t) -> p k t", t=P)
                             ).then_inc(read_act, 1)
            act.wait_ge(vec_ready, 1)
            act.activation(m.cond[:, :, :], m.vec_b[:, VEC_B["c"]:VEC_B["c"] + 16].rearrange("p (i k) -> p i k", k=KB),
                           ACT.Silu).then_inc(silu_done, 1)

        @block.gpsimd
        def _(pool):
            pool.memset(m.ident[:, :], 0.0)
            pool.memset(m.ones[:, :], 1.0)
            pool.memset(m.neg_half[:, :], -0.5)
            pool.drain()
            pool.affine_select(out=m.ident[:, :], in_=m.ident[:, :], compare_op=ALU.not_equal, fill=1.0, base=0,
                               pattern=[[-1, P]], channel_multiplier=1).then_inc(ident_ready, 1)

        @block.tensor
        def _(pe):
            pe.wait_ge(ident_ready, 1)
            pe.wait_ge(rows_loaded, 16 * n_small)
            pe.transpose(m.psum[:, 4 * BANK:4 * BANK + P], rows[:, 0, :], m.ident[:, :])
            pe.transpose(m.psum[:, 4 * BANK + P:4 * BANK + 2 * P], rows[:, 1, :], m.ident[:, :]).then_inc(vec_turned, 1)
            for i, (t, h) in enumerate(batches):
                pe.wait_ge(x_loaded[t], 16)
                if i >= 4:
                    pe.wait_ge((read_act, read_dve)[i % 2], (i - 4) // 2 + 1)
                for k in range(4):
                    c = (4 * h + k) * P
                    last = pe.transpose(m.psum[:, (i % 4) * BANK + k * P:(i % 4) * BANK + (k + 1) * P],
                                        xin_tok[:, t, c:c + P], m.ident[:, :])
                last.then_inc(turned, 1)

        @block.vector
        def _(dve):
            dve.memset(rows[:, :, :], 0.0).then_inc(rows_zeroed, 1)
            dve.wait_ge(vec_turned, 1)
            dve.tensor_copy(m.vec_a[:, :], m.psum[:, 4 * BANK:4 * BANK + P])
            dve.tensor_copy(m.vec_b[:, :], m.psum[:, 4 * BANK + P:4 * BANK + 2 * P]).then_inc(vec_ready, 1)
            for i, (t, h) in enumerate(batches):
                if i % 2 == 1:
                    dve.wait_ge(turned, i + 1)
                    dve.tensor_copy(x[:, 4 * h:4 * h + 4, t * P:(t + 1) * P],
                                    m.psum[:, (i % 4) * BANK:(i % 4 + 1) * BANK].rearrange("p (k t) -> p k t", t=P)
                                    ).then_inc(read_dve, 1)


def adaln(m, a, sem, l, slots, rows, banks, sums_at):
    blocks, n_slots = 6 * D // BANK, len(slots)
    halves = 2 * blocks
    loaded = [sem(f"ada{l}_loaded{i}") for i in range(n_slots)]
    used, row_done, row_read, turned = (sem(f"ada{l}_" + n) for n in ("used", "row_done", "row_read", "turned"))
    w = (a["l0_ada_w"], a["l1_ada_w"])[l].rearrange("(h k p) n -> p h k n", p=P, h=2)
    t = Memory()

    def load(sp, r, x):
        sp.dma_start(slots[x % n_slots][:, :, :], w[:, x % 2, :, ds(r * 4 * BANK + (x // 2) * BANK, BANK)]
                     ).then_inc(loaded[x % n_slots], 16)

    def ahead(sp):
        for x in range(n_slots):
            load(sp, 0, x)

    def loads(sp):
        for x in range(n_slots, 8):
            wait_value(m, sp, used, x - n_slots + 1)
            load(sp, 0, x)
        with sp.Fori(1, halves // 8) as r:
            for x in range(8):
                wait_value(m, sp, used, r * 8 + (x - n_slots + 1))
                load(sp, r, x)

    def products(pe):
        with pe.Fori(0, blocks // 4) as r:
            def turn(i):
                pe.wait_ge(row_read, r * 4 + (i + 1))
                for n in range(4):
                    last = pe.matmul(m.psum[:, ds(r * 32 + (sums_at + i * 8 + n * 2), 2)],
                                     rows[i % 2][:, n * P:(n + 1) * P], m.ident[0:2, 0:2], start=True, stop=True)
                last.then_inc(turned, 1)

            for i in range(4):
                pe.wait_ge(row_read, r * 4 + (i - 1 if i else 0))
                for x in (2 * i, 2 * i + 1):
                    pe.wait_ge(loaded[x % n_slots], r * (16 * 8 // n_slots) + 16 * (x // n_slots + 1))
                    for k in range(4):
                        kk = 4 * (x % 2) + k
                        last = pe.matmul(m.psum[0:2, banks[i % 2] * BANK:(banks[i % 2] + 1) * BANK], m.cond[:, :, kk],
                                         slots[x % n_slots][:, k, :], start=(kk == 0), stop=(kk == KB - 1))
                    last.then_inc(used, 1)
                if i >= 1:
                    turn(i - 1)
            turn(3)

    def copies(act):
        with act.Fori(0, blocks // 4) as r:
            for i in range(4):
                act.wait_ge(used, r * 8 + (2 * i + 2))
                if i >= 2:
                    act.wait_ge(turned, r * 4 + (i - 1))
                else:
                    act.wait_ge(turned, r * 4)
                act.copy(rows[i % 2][:, :], m.psum[0:2, banks[i % 2] * BANK:(banks[i % 2] + 1) * BANK]
                         ).then_inc(row_read, 1)

    def vectors(dve):
        dve.wait_ge(turned, blocks)
        at = VEC_A[f"l{l}_ada_b"]
        bias = m.vec_a[:, at:at + 48].unsqueeze(2).broadcast_to([P, 48, 2])
        sums = m.psum[:, sums_at:sums_at + 96].rearrange("p (n c) -> p n c", c=2)
        dve.tensor_tensor(m.mod[l][:, :, :], sums, bias, ALU.add)
        dve.drain()
        for i in range(2):
            at = VEC_A[f"l{l}_norm{i + 1}"]
            gain = m.vec_a[:, at:at + 8].unsqueeze(2).broadcast_to([P, KB, 2])
            c = (1 + 3 * i) * KB
            dve.scalar_tensor_tensor(m.norm_scale[l][i][:, :, :], m.mod[l][:, c:c + KB, :], 1.0, gain, ALU.add, ALU.mult)

    t.ahead, t.loads, t.products, t.copies, t.vectors = ahead, loads, products, copies, vectors
    return t


def modulation(nc, m, sem, ada):
    lam_rows = m.lam_rows
    put = placer(m, "small", m.scratch_at + 6 * 16384 + 1024, m.end)
    lam_prod = put("lam_prod", [P, 2, HD])
    lam_sum = put("lam_sum", [P, 4])
    y, s, s2, acc, t0 = (put(n, [P, 8]) for n in ("y", "s", "s2", "acc", "t0"))
    exp_done, lam_summed, abs_ready = (sem(n) for n in ("exp_done", "lam_summed", "abs_ready"))
    with nc.Block() as block:
        @block.sync
        def _(sp):
            ada.loads(sp)

        @block.tensor
        def _(pe):
            ada.products(pe)

        @block.scalar
        def _(act):
            act.wait_ge(lam_summed, 1)
            act.activation(lam_sum[:, 2:4], lam_sum[:, 0:2], ACT.Exp).then_inc(exp_done, 1)
            act.wait_ge(abs_ready, 1)
            act.activation(y[:, :], y[:, :], ACT.Exp, scale=-1.0).then_inc(exp_done, 1)
            ada.copies(act)

        @block.vector
        def _(dve):
            for i in range(2):
                dve.tensor_tensor(lam_prod[:, i, :], lam_rows[:, 2 * i, :], lam_rows[:, 2 * i + 1, :], ALU.mult)
            dve.drain()
            dve.tensor_reduce(lam_sum[:, 0:2], lam_prod[:, :, :], AX.X, ALU.add).then_inc(lam_summed, 1)
            fb = VEC_B["l0_fwd_ba"]
            dve.tensor_scalar(m.gate_bias[:, :], m.vec_b[:, fb:fb + 16], 0.5, None, ALU.mult)
            dve.tensor_scalar(m.subln[:, 0:1], m.vec_b[:, VEC_B["subln"]:VEC_B["subln"] + 1], 1.0 - LAM_INIT, None,
                              ALU.mult)
            lam = m.vec_b[:, VEC_B["l0_fwd_lam"]:VEC_B["l0_fwd_lam"] + 8]
            dve.tensor_scalar(t0[:, :], lam, -1.0, None, ALU.mult)
            dve.drain()
            dve.tensor_tensor(y[:, :], lam, t0[:, :], ALU.max).then_inc(abs_ready, 1)
            dve.wait_ge(exp_done, 2)
            dve.tensor_scalar(s[:, :], y[:, :], 2.0, None, ALU.add)
            dve.drain()
            dve.reciprocal(s2[:, :], s[:, :])
            dve.drain()
            dve.tensor_tensor(s[:, :], y[:, :], s2[:, :], ALU.mult)
            dve.drain()
            dve.tensor_tensor(s2[:, :], s[:, :], s[:, :], ALU.mult)
            dve.memset(acc[:, :], 1.0 / 17)
            for n in (15, 13, 11, 9, 7, 5, 3, 1):
                dve.drain()
                dve.tensor_tensor(acc[:, :], acc[:, :], s2[:, :], ALU.mult)
                dve.drain()
                dve.tensor_scalar(acc[:, :], acc[:, :], 1.0 / n, None, ALU.add)
            dve.tensor_scalar(t0[:, :], t0[:, :], 0.0, None, ALU.max)
            dve.drain()
            dve.tensor_tensor(acc[:, :], acc[:, :], s[:, :], ALU.mult)
            dve.drain()
            dve.scalar_tensor_tensor(acc[:, :], acc[:, :], 2.0, t0[:, :], ALU.mult, ALU.add)
            dve.drain()
            dve.tensor_scalar(m.decay[:, 0, :], acc[:, :], -4.0, None, ALU.mult)
            dve.tensor_scalar(m.decay[:, 1, :], acc[:, :], 2.0, None, ALU.mult)
            dve.tensor_tensor(lam_sum[:, 0:1], lam_sum[:, 3:4], lam_sum[:, 2:3], ALU.subtract)
            dve.drain()
            dve.tensor_scalar(m.neg_lambda[:, 0:1], lam_sum[:, 0:1], -LAM_INIT, None, ALU.add)
            ada.vectors(dve)


SPANS = ((0, LAT, 0), (LAT, TOK, 1))
CHUNKS = ((0, BANK), (BANK, 2 * BANK), (2 * BANK, TOK))


def modulated_norm(nc, m, a, sem, l, i, x, h, ahead=None):
    n = f"n{l}{i}"
    squared, square_sum, summed, mean_ready, rstd_ready, spread, scaled = (sem(f"{n}_{s}") for s in (
        "squared", "square_sum", "summed", "mean", "rstd", "spread", "scaled"))
    ssq_ps = m.psum[:, 7 * BANK:7 * BANK + NT]
    spread_ps = m.psum[:, 0:TOK]
    with nc.Block() as block:
        if ahead:
            @block.sync
            def _(sp):
                ahead(sp)

        @block.scalar
        def _(act):
            for k in range(KB):
                act.activation(h[:, k, :], x[:, k, :], ACT.Square).then_inc(squared, 1)
            for k in range(KB):
                act.wait_ge(scaled, k + 1)
                act.activation(h[:, k, 0:LAT], h[:, k, 0:LAT], ACT.Identity, bias=m.mod[l][:, 3 * i * KB + k, 0:1],
                               scale=m.norm_scale[l][i][:, k, 0:1])

        @block.tensor
        def _(pe):
            pe.wait_ge(square_sum, 1)
            for t in range(NT):
                last = pe.matmul(ssq_ps[:, t:t + 1], h[:, 0, t * P:(t + 1) * P], m.ones[:, 0:1], start=True, stop=True)
            last.then_inc(summed, 1)
            pe.wait_ge(rstd_ready, 1)
            for t in range(NT):
                last = pe.matmul(spread_ps[:, t * P:(t + 1) * P], m.rstd[:, t:t + 1].broadcast_to([P, P]),
                                 m.ident[:, :], start=True, stop=True)
            last.then_inc(spread, 1)

        @block.vector
        def _(dve):
            for k in range(1, KB):
                dve.wait_ge(squared, k + 1)
                last = dve.tensor_tensor(h[:, 0, :], h[:, 0, :], h[:, k, :], ALU.add)
                if k < KB - 1:
                    dve.drain()
            last.then_inc(square_sum, 1)
            dve.wait_ge(summed, 1)
            dve.tensor_scalar(m.ssq[:, 0:NT], ssq_ps, 1.0 / D, EPS, ALU.mult, ALU.add).then_inc(mean_ready, 1)
            dve.wait_ge(spread, 1)
            for k in range(KB):
                dve.tensor_tensor(h[:, k, :], x[:, k, :], spread_ps, ALU.mult).then_inc(scaled, 1)

        @block.gpsimd
        def _(pool):
            pool.wait_ge(mean_ready, 1)
            pool.tensor_tensor(m.rstd[:, 0:NT], m.ssq[:, 0:NT], m.neg_half[:, 0:NT], ALU.pow).then_inc(rstd_ready, 1)
            for k in range(KB):
                pool.wait_ge(scaled, k + 1)
                pool.tensor_scalar(h[:, k, LAT:TOK], h[:, k, LAT:TOK], m.norm_scale[l][i][:, k, 1:2],
                                   m.mod[l][:, 3 * i * KB + k, 1:2], ALU.mult, ALU.add)


def recurrent_weights(nc, m, a, sem):
    pre = Memory()
    put = placer(m, "lruw", m.scratch_at + 21504, m.end)
    pre.w_x, pre.w_g = put("w_x", [P, KB, P]), put("w_g", [P, KB, P])
    pre.end = put.pos[0]
    pre.wx_loaded, pre.wg_loaded = sem("lru_wx_loaded"), sem("lru_wg_loaded")
    w_in = a["l0_w_in"].rearrange("(k p) n -> p k n", p=P)
    pre.load_x = lambda sp, c: sp.dma_start(pre.w_x[:, :, :], w_in[:, :, ds(c * P + 768, P)]).then_inc(pre.wx_loaded, 16)
    pre.load_g = lambda sp, c: sp.dma_start(pre.w_g[:, :, :], w_in[:, :, ds(c * P + (768 + LRU), P)]
                                            ).then_inc(pre.wg_loaded, 16)
    return pre


def recurrent_branch(nc, m, a, sem, x, h, cat, x_dram, pre, attn_ahead):
    w_x, w_g = pre.w_x, pre.w_g
    put = placer(m, "lru", pre.end, m.end)
    w_gate = put("w_gate", [P, 4, P])
    xb = put("xb", [P, TOK + 8])
    gb, xc, gl, hsum = (put(n, [P, TOK]) for n in ("gb", "xc", "gl", "hsum"))
    rt, it, av, bv, hv = ([put(f"{n}{d}", [P, TOK]) for d in range(2)] for n in ("rt", "it", "av", "bv", "hv"))
    last_h = put("last_h", [P, 2, LC])
    L0, C0 = 1, LAT + 4
    segments = ((L0, 0, LAT), (C0, LAT, CTX))
    names = ("x_saved", "gates_loaded", "gates_zeroed", "pad_zeroed", "task_done", "task_read", "xb_ready",
             "conv_done", "decay_ready", "root_ready", "gelu_square", "gelu_inner", "gelu_tanh", "rec_done",
             "last_ready", "last_stored")
    s = {n: sem("lru_" + n) for n in names}
    s["wx_loaded"], s["wg_loaded"] = pre.wx_loaded, pre.wg_loaded
    TASKS = 6

    with nc.Block() as block:
        @block.sync
        def _(sp):
            def gates(c):
                for i, w in enumerate((a["l0_fwd_wa"], a["l0_fwd_wi"], a["l0_bwd_wa"], a["l0_bwd_wi"])):
                    for b in range(2):
                        blk = w[ds(c * 2 + b, 1)].rearrange("o i j -> (o i) j")
                        sp.dma_start(w_gate[64 * b:64 * b + 64, i, 64 * b:64 * b + 64], blk
                                     ).then_inc(s["gates_loaded"], 16)

            sp.wait_ge(s["gates_zeroed"], 1)
            gates(0)
            sp.dma_start(x_dram.rearrange("p (k t) -> p k t", t=TOK), x[:, :, :]).then_inc(s["x_saved"], 16)
            attn_ahead(sp)
            with sp.Fori(0, LC - 1) as c:
                wait_value(m, sp, s["task_done"], c * TASKS + 1)
                pre.load_x(sp, c + 1)
                wait_value(m, sp, s["task_done"], c * TASKS + 2)
                pre.load_g(sp, c + 1)
                wait_value(m, sp, s["task_done"], c * TASKS + TASKS)
                gates(c + 1)
            sp.wait_ge(s["last_ready"], LC)
            with nc.allow_non_contiguous_dma(reason="the last states, 512 floats each"):
                sp.dma_start(a["new_l0_fwd"].rearrange("b (c p) -> p (b c)", p=P), last_h[:, 0, :]).then_inc(s["last_stored"], 16)
                sp.dma_start(a["new_l0_bwd"].rearrange("b (c p) -> p (b c)", p=P), last_h[:, 1, :]).then_inc(s["last_stored"], 16)
            sp.wait_ge(s["last_stored"], 32)
            sp.wait_ge(s["x_saved"], 16)

        @block.gpsimd
        def _(pool):
            pool.memset(w_gate[:, :, :], 0.0).then_inc(s["gates_zeroed"], 1)
            pool.memset(xb[:, :], 0.0).then_inc(s["pad_zeroed"], 1)

        @block.tensor
        def _(pe):
            with pe.Fori(0, LC) as c:
                for n in range(TASKS):
                    at = 3 * BANK * (n % 2)
                    if n < 2:
                        pe.wait_ge((s["wx_loaded"], s["wg_loaded"])[n], c * 16 + 16)
                    elif n == 2:
                        pe.wait_ge(s["conv_done"], c + 1)
                        pe.wait_ge(s["gates_loaded"], c * 128 + 128)
                    if n >= 2:
                        pe.wait_ge(s["task_read"], c * TASKS + (n - 1))
                    elif n == 1:
                        pe.wait_ge(s["task_read"], c * TASKS)
                    else:
                        pe.wait_ge(s["task_read"], c * TASKS)
                    for lo, hi in CHUNKS:
                        out = m.psum[:, at + lo:at + hi]
                        if n < 2:
                            for k in range(KB):
                                last = pe.matmul(out, (w_x, w_g)[n][:, k, :], h[:, k, lo:hi],
                                                 start=(k == 0), stop=(k == KB - 1))
                        else:
                            last = pe.matmul(out, w_gate[:, n - 2, :], xc[:, lo:hi], start=True, stop=True)
                    last.then_inc(s["task_done"], 1)

        @block.scalar
        def _(act):
            act.wait_ge(s["pad_zeroed"], 1)
            with act.Fori(0, LC) as c:
                act.wait_ge(s["task_done"], c * TASKS + 1)
                act.wait_ge(s["conv_done"], c)
                act.copy(xb[:, L0:L0 + LAT], m.psum[:, 0:LAT])
                act.copy(xb[:, C0:C0 + CTX], m.psum[:, LAT:TOK]).then_inc(s["xb_ready"], 1)
                act.drain()
                act.sem_inc(s["task_read"], 1)
                act.wait_ge(s["task_done"], c * TASKS + 2)
                act.wait_ge(s["rec_done"], c)
                act.copy(gb[:, :], m.psum[:, 3 * BANK:3 * BANK + TOK]).then_inc(s["task_read"], 1)
                act.drain()
                act.activation(gl[:, :], gb[:, :], ACT.Square).then_inc(s["gelu_square"], 1)
                for d in range(2):
                    act.wait_ge(s["task_done"], c * TASKS + (3 + 2 * d))
                    act.activation(rt[d][:, :], m.psum[:, 0:TOK], ACT.Tanh, scale=0.5,
                                   bias=m.gate_bias[:, ds(c + 8 * d, 1)]).then_inc(s["task_read"], 1)
                    act.wait_ge(s["task_done"], c * TASKS + (4 + 2 * d))
                    act.activation(it[d][:, :], m.psum[:, 3 * BANK:3 * BANK + TOK], ACT.Tanh, scale=0.5,
                                   bias=m.gate_bias[:, ds(c + (8 * d + 4), 1)]).then_inc(s["task_read"], 1)
                act.drain()
                for d in range(2):
                    act.activation(av[d][:, :], rt[d][:, :], ACT.Exp, bias=m.decay[:, 0, ds(c + 4 * d, 1)],
                                   scale=m.decay[:, 0, ds(c + 4 * d, 1)]).then_inc(s["decay_ready"], 1)
                act.drain()
                for d in range(2):
                    act.activation(rt[d][:, :], rt[d][:, :], ACT.Tanh, bias=m.decay[:, 1, ds(c + 4 * d, 1)],
                                   scale=m.decay[:, 1, ds(c + 4 * d, 1)])
                act.drain()
                act.wait_ge(s["gelu_inner"], c + 1)
                act.activation(gl[:, :], gl[:, :], ACT.Tanh, scale=GELU_C).then_inc(s["gelu_tanh"], 1)
                for d in range(2):
                    act.activation(bv[d][:, :], rt[d][:, :], ACT.Sqrt).then_inc(s["root_ready"], 1)

        @block.vector
        def _(dve):
            conv = lambda j: m.vec_b[:, ds(j, 1)]
            with dve.Fori(0, LC) as c:
                dve.wait_ge(s["xb_ready"], c + 1)
                for pad, at, n in segments:
                    dve.tensor_scalar(xc[:, at:at + n], xb[:, pad - 1:pad - 1 + n], conv(c), conv(c + VEC_B["conv_b"]),
                                      ALU.mult, ALU.add)
                for j in range(1, 4):
                    dve.drain()
                    for pad, at, n in segments:
                        last = dve.scalar_tensor_tensor(xc[:, at:at + n], xb[:, pad - 1 + j:pad - 1 + j + n],
                                                        conv(c + 4 * j), xc[:, at:at + n], ALU.mult, ALU.add)
                last.then_inc(s["conv_done"], 1)
                dve.wait_ge(s["gelu_square"], c + 1)
                dve.tensor_scalar(gl[:, :], gl[:, :], 0.044715, 1.0, ALU.mult, ALU.add)
                dve.drain()
                dve.tensor_tensor(gl[:, :], gl[:, :], gb[:, :], ALU.mult).then_inc(s["gelu_inner"], 1)
                for d in range(2):
                    dve.wait_ge(s["decay_ready"], c * 2 + (d + 1))
                    dve.scalar_tensor_tensor(it[d][:, :], it[d][:, :], 1.0, xc[:, :], ALU.add, ALU.mult)
                    dve.drain()
                    dve.scalar_tensor_tensor(it[d][:, :], av[d][:, :], 1.0, it[d][:, :], ALU.add, ALU.mult)
                dve.wait_ge(s["gelu_tanh"], c + 1)
                dve.scalar_tensor_tensor(gl[:, :], gl[:, :], 1.0, gb[:, :], ALU.add, ALU.mult)
                for d in range(2):
                    dve.wait_ge(s["root_ready"], c * 2 + (d + 1))
                    dve.scalar_tensor_tensor(bv[d][:, :], bv[d][:, :], 0.5, it[d][:, :], ALU.mult, ALU.mult)
                    dve.drain()
                    state = m.vec_b[:, ds(c + (VEC_B["state_l0_fwd"] + 4 * d), 1)]
                    lat = (slice(0, LAT), slice(LAT, TOK)) if d == 0 else (slice(LAT - 1, None, -1), slice(TOK - 1, LAT - 1, -1))
                    dve.tensor_tensor_scan(hv[d][:, lat[0]], av[d][:, lat[0]], bv[d][:, lat[0]], state, ALU.mult, ALU.add)
                    dve.tensor_tensor_scan(hv[d][:, lat[1]], av[d][:, lat[1]], bv[d][:, lat[1]], 0.0, ALU.mult, ALU.add)
                dve.drain()
                dve.tensor_copy(last_h[:, 0, ds(c, 1)], hv[0][:, TOK - 1:TOK])
                dve.tensor_copy(last_h[:, 1, ds(c, 1)], hv[1][:, LAT:LAT + 1]).then_inc(s["last_ready"], 1)
                dve.tensor_tensor(hsum[:, :], hv[0][:, :], hv[1][:, :], ALU.add)
                dve.drain()
                dve.wait_ge(s["x_saved"], 16)
                dve.scalar_tensor_tensor(cat[:, ds(c + 4, 1), :].rearrange("p o t -> p (o t)"), hsum[:, :], 0.5, gl[:, :],
                                         ALU.mult, ALU.mult).then_inc(s["rec_done"], 1)
                dve.drain()


def attention_weights(nc, m, a, sem, l):
    pre = Memory()
    put = placer(m, f"attnw{l}", m.scratch_at, m.end)
    pre.w = put("w", [P, KB, (384, 768)[l]])
    pre.cos, pre.sin = put("cos", [P, LT, 2, HD]), put("sin", [P, LT, 2, HD])
    pre.gains = put("gains", [P, 2, HD])
    pre.end = put.pos[0]
    pre.w_loaded, pre.tables_loaded = sem(f"a{l}_w_loaded"), sem(f"a{l}_tables_loaded")
    w_in = (a["l0_w_in"], a["l1_w_in"])[l].rearrange("(k p) n -> p k n", p=P)
    pieces = [[(0, 256, 0, 256), (256, 64, 512, 64), (320, 64, 640, 64)],
              [(0, 128, 0, 128), (128, 128, 512, 128), (256, 128, 1024, 128), (384, 128, 1536, 128),
               (512, 256, 2048, 256)]][l]
    pre.pieces = len(pieces)

    def load(sp, j):
        for at, width, first, step in pieces:
            sp.dma_start(pre.w[:, :, at:at + width], w_in[:, :, ds(j * step + first, width)]).then_inc(pre.w_loaded, 16)

    def ahead(sp):
        load(sp, 0)
        for tab, src in ((pre.cos, a["rope_cos"]), (pre.sin, a["rope_sin"])):
            for i in range(2):
                sp.dma_start(tab[:, :, i, :], src.rearrange("(t p) d -> p t d", p=P)).then_inc(pre.tables_loaded, 16)
        for i, g in enumerate(((a["l0_q_gain"], a["l0_k_gain"]), (a["l1_q_gain"], a["l1_k_gain"]))[l]):
            sp.dma_start(pre.gains[:, i, :], g.unsqueeze(0).broadcast_to([P, HD])).then_inc(pre.tables_loaded, 16)

    pre.load, pre.ahead = load, ahead
    return pre


def attention(nc, m, a, sem, l, x, h, cat, x_dram, pre, out_ahead):
    groups = (2, 4)[l]
    nq, nk, dv = 4, (1, 4)[l], (64, 128)[l]
    vw = (64, 256)[l]
    per_tile = (4, 2)[l]
    maps = (1, 2)[l]
    units = NT * per_tile
    nmaps = units * maps
    nz = nq + nk
    zw = nz * HD + (vw if l == 0 else 0)
    w_cols = nz * HD + vw
    ck, cv = ((a["cache_l0_k"][0], a["cache_l0_v"][0]), (a["cache_l1_k"][0], a["cache_l1_v"][0]))[l]

    put = placer(m, f"attn{l}", pre.end, m.end)
    w, cos_t, sin_t, gains = pre.w, pre.cos, pre.sin, pre.gains
    vt = put("v", [P, KT + 1, vw])
    ks = put("ks", [P, nk, KEYS + CTX], F32R)
    qtok = put("qtok", [P, NT, nq * HD])
    e_at = put.pos[0]
    e = [put(f"e{i}", [P, KEYS]) for i in range(3)]
    pt = [put(f"pt{i}", [P, KEYS]) for i in range(2)]
    o_at = put.pos[0]
    o = put("o", [P, NT, 4 * HD])
    qst_at = put.pos[0]
    qst = [put(f"qst{i}", [P, nq, 2, P], F32R) for i in range(2)]
    qq = put("qq", [P, nq, 3, HD])
    khl = [put(f"khl{i}", [P, nk, 2, HD]) for i in range(2)]
    z_at = put.pos[0]
    za, zb, zc = (put(n, [P, nz * HD]) for n in ("za", "zb", "zc"))
    if l == 1:
        e = [e[0], e[1], m.tensor("attn1_e3", [P, KEYS], F32, z_at), e[2]]
    kc = za[:, 0:PT_TILES * nk * HD].rearrange("p (t c) -> p t c", t=PT_TILES)
    sq = qq[:, :, :, :].rearrange("p n v d -> p (n v d)")[:, 0:nz * HD]
    w_hi = m.tensor(f"attn{l}_w_hi", [P, KB, w_cols], F32R, e_at)
    w_lo = m.tensor(f"attn{l}_w_lo", [P, KB, w_cols], F32R, m.scratch_at)
    hs = [m.tensor(f"attn{l}_hs{i}", [P, 2, KB, P], F32R, at) for i, at in enumerate((o_at, qst_at))]
    kf = put("kf", [P, nk * HD])
    neg_max, sums, inv, ratio, red = (put(n, [P, 40]) for n in ("neg_max", "sums", "inv", "ratio", "red"))

    names = ("cache_loaded", "x_saved", "x_back", "w_used", "z_done", "v_done", "squared", "ssq", "rstd",
             "z_read", "v_copied", "k_split", "turned", "turn_read", "q_split", "scored", "maxed", "expd",
             "mixed", "pv_done", "o_read", "o_squared", "o_mean", "h_high", "h_split", "w_high", "w_split",
             "o_rstd", "o_normed", "k_stored", "k_new")
    s = {n: sem(f"a{l}_" + n) for n in names}
    s["w_loaded"], s["tables_loaded"] = pre.w_loaded, pre.tables_loaded

    turns_k = KT + 1
    TURNS = turns_k + 2 * NT + 3 * (units - per_tile) + per_tile + 6
    turn_bank = lambda n: (6 + n % 2) * BANK
    score_at = lambda n: (n % 2) * 3 * BANK

    def program(make):
        for t in range(NT):
            make["project"](t)
            if t == 1:
                make["cache_keys"]()
            if t >= 1:
                make["turn_keys"](t - 1 + PT_TILES)
        make["turn_keys"](NT - 1 + PT_TILES)
        make["stage"](0)
        for i in range(maps):
            make["scores"](0, i)
        for u in range(units + 2):
            if u + 1 < units:
                make["scores"](u + 1, 0)
            if u % per_tile == 0 and u // per_tile + 1 < NT:
                make["stage"](u // per_tile + 1)
            if 1 <= u <= units:
                make["turn_probs"](u - 1, 0)
            if u + 1 < units and maps == 2:
                make["scores"](u + 1, 1)
            if 1 <= u <= units:
                make["turn_probs"](u - 1, 1)
            if u >= 2:
                make["values"](u - 2)
        make["turn_out"]()

    def key_span(u):
        return (0, KEYS, range(KT)) if u // per_tile < LT else (KEYS, KEYS + CTX, range(KT, KT + 1))

    def turn_parts(n, part):
        return range(0, n, 4)[:2] if part == 0 else range(0, n, 4)[2:]

    def unit_maps(u):
        i = u % per_tile
        return [(i, 0)] if l == 0 else [(i, i), (2 + i, 2 + i)]

    NORM_PARTS = ((0, 7), (7, NT))
    osum = ratio[:, 2 * NT:4 * NT]
    o_waste = zc[:, nz * HD - dv:nz * HD]

    with nc.Block() as block:
        @block.sync
        def _(sp):
            if l == 1:
                sp.dma_start(x_dram.rearrange("p (k t) -> p k t", t=TOK), x[:, :, :]).then_inc(s["x_saved"], 16)
            k_new, v_new = ((a["new_l0_k"], a["new_l0_v"]), (a["new_l1_k"], a["new_l1_v"]))[l]


            def group(j, last):
                wait_value(m, sp, s["pv_done"], j * units)
                for t in range(PT_TILES):
                    rows = slice(t * P, (t + 1) * P)
                    if l == 0:
                        ksrc = ck[rows, ds(j, 1), :].rearrange("p o d -> p (o d)")
                        vsrc = cv[rows, ds(j, 1), :].rearrange("p o d -> p (o d)")
                        kdst = kc[:, t, :]
                    else:
                        ksrc = ck[rows, :, ds(j * 2, 2), :].rearrange("p i h d -> p i (h d)")
                        vsrc = cv[rows, ds(j * 2, 2), :].rearrange("p h d -> p (h d)")
                        kdst = kc[:, t, :].rearrange("p (i c) -> p i c", i=2)
                    sp.dma_start(kdst, ksrc).then_inc(s["cache_loaded"], 16)
                    sp.dma_start(vt[:, t, :], vsrc).then_inc(s["cache_loaded"], 16)
                wait_value(m, sp, s["w_used"], j + 1)
                if last:
                    out_ahead(sp)
                else:
                    pre.load(sp, j + 1)
                wait_value(m, sp, s["k_new"], j + 1)
                wait_value(m, sp, s["v_copied"], j * NT + NT)
                if l == 0:
                    sp.dma_start(k_new[0, :, ds(j, 1), :].rearrange("p o d -> p (o d)"), kf[:, :]).then_inc(s["k_stored"], 16)
                    sp.dma_start(v_new[0, :, ds(j, 1), :].rearrange("p o d -> p (o d)"), vt[:, KT, :]).then_inc(s["k_stored"], 16)
                else:
                    sp.dma_start(k_new[0, :, :, ds(j * 2, 2), :].rearrange("p i h d -> p i (h d)"),
                                 kf[:, :].rearrange("p (i c) -> p i c", i=2)).then_inc(s["k_stored"], 16)
                    sp.dma_start(v_new[0, :, ds(j * 2, 2), :].rearrange("p h d -> p (h d)"), vt[:, KT, :]
                                 ).then_inc(s["k_stored"], 16)
            with sp.Fori(0, groups - 1) as j:
                group(j, False)
            with sp.Fori(groups - 1, groups) as j:
                group(j, True)
            sp.wait_ge(s["w_used"], groups)
            sp.dma_start(h[:, :, :], x_dram.rearrange("p (k t) -> p k t", t=TOK)).then_inc(s["x_back"], 16)
            sp.wait_ge(s["x_back"], 16)
            sp.wait_ge(s["k_stored"], 32 * groups)
            if l == 1:
                sp.wait_ge(s["x_saved"], 16)

        @block.gpsimd
        def _(pool):
            with pool.Fori(0, groups) as j:
                for t in range(NT):
                    wait_value(m, pool, s["ssq"], j * NT + (t + 1))
                    pool.tensor_tensor(m.rstd[:, 0:nz], m.ssq[:, 0:nz], m.neg_half[:, 0:nz], ALU.pow).then_inc(s["rstd"], 1)
                if l == 1:
                    for i, (lo, hi) in enumerate(NORM_PARTS):
                        wait_value(m, pool, s["o_mean"], j * 2 + (i + 1))
                        pool.tensor_tensor(m.rstd[:, 2 * lo:2 * hi], m.ssq[:, 2 * lo:2 * hi], m.neg_half[:, 2 * lo:2 * hi],
                                           ALU.pow).then_inc(s["o_rstd"], 1)

        @block.tensor
        def _(pe):
            with pe.Fori(0, groups) as j:
                turn, uses = [0], []

                def next_bank(output=None):
                    n = len(uses)
                    if n >= 2:
                        what, count = uses[n - 2]
                        if what == "output":
                            pe.wait_ge(s["o_read"], j * units + count)
                        else:
                            pe.wait_ge(s["turn_read"], j * TURNS + count)
                    uses.append(("output", output + 1) if output is not None else ("transpose", turn[0] + 1))
                    return turn_bank(n)

                def next_turn():
                    at = next_bank()
                    turn[0] += 1
                    return at

                def turn_keys(i):
                    pe.wait_ge(s["k_split"], j * turns_k + (i + 1))
                    at = next_turn()
                    for n in range(nk):
                        last = pe.transpose(m.psum[:, at + n * P:at + (n + 1) * P],
                                            khl[i % 2][:, n, :, :].rearrange("p v d -> p (v d)"), m.ident[:, :])
                    last.then_inc(s["turned"], 1)

                def cache_keys():
                    pe.wait_ge(s["turn_read"], j * TURNS)
                    for i in range(PT_TILES):
                        turn_keys(i)

                def project(t):
                    pe.wait_ge(s["h_split"], j * NT + (t + 1))
                    if t == 0:
                        pe.wait_ge(s["expd"], j * nmaps)
                    if t >= 2:
                        pe.wait_ge(s["z_read"], j * NT + (t - 1))
                        pe.wait_ge(s["v_copied"], j * NT + (t - 1))
                    z = m.psum[:, (t % 2) * BANK:(t % 2) * BANK + zw]


                    def product(out, lo, hi):
                        for k in range(KB):
                            if t == 0 and lo == 0:
                                pe.wait_ge(s["w_split"], j * KB + (k + 1))
                            for n, (part, right) in enumerate(((0, w_hi[:, k, lo:hi]), (0, w_lo[:, k, lo:hi]),
                                                               (1, w_hi[:, k, lo:hi]))):
                                last = pe.matmul(out, hs[t % 2][:, part, k, :], right, start=(k == 0 and n == 0),
                                                 stop=(k == KB - 1 and n == 2))
                        return last

                    product(z, 0, zw).then_inc(s["z_done"], 1)
                    if l == 1:
                        v = m.psum[:, (2 + t % 2) * BANK:(2 + t % 2) * BANK + vw]
                        product(v, zw, zw + vw).then_inc(s["v_done"], 1)
                    if t == NT - 1:
                        pe.wait_ge((s["z_done"], s["v_done"])[l], j * NT + NT)
                        pe.sem_inc(s["w_used"], 1)

                def stage(qt):
                    pe.wait_ge(s["q_split"], j * NT + (qt + 1))
                    for half in range(2):
                        at = next_turn()
                        for i in range(2):
                            n = 2 * half + i
                            flat = qq[:, n, :, :].rearrange("p v d -> p (v d)")
                            for v in range(2):
                                last = pe.transpose(m.psum[:, at + (2 * i + v) * P:at + (2 * i + v + 1) * P],
                                                    flat[:, v * HD:v * HD + P], m.ident[:, :])
                        last.then_inc(s["turned"], 1)
                    if qt == 0:
                        pe.wait_ge(s["z_read"], j * NT + NT)
                        pe.wait_ge(s["v_copied"], j * NT + NT)

                staged = {}

                def scores(u, which):
                    lo, hi, _ = key_span(u)
                    for i, (qm, km) in [(which, unit_maps(u)[which])]:
                        n = u * maps + i
                        if u % per_tile == 0 and i == 0:
                            pe.wait_ge(s["turn_read"], j * TURNS + staged[u // per_tile])
                        if n >= 2:
                            pe.wait_ge(s["expd"], j * nmaps + (n - 1))
                        at = score_at(n)
                        col = lo
                        while col < hi:
                            into = at + col - lo
                            step = min(BANK - into % BANK, hi - col)
                            for v in range(2):
                                last = pe.matmul(m.psum[:, into:into + step], qst[(u // per_tile) % 2][:, qm, v, :],
                                                 ks[:, km, col:col + step], start=(v == 0), stop=(v == 1))
                            col += step
                        last.then_inc(s["scored"], 1)

                def turn_probs(u, part):
                    _, _, tiles = key_span(u)
                    pe.wait_ge(s["expd"], j * nmaps + (u + 1) * maps)
                    if l == 1:
                        pe.wait_ge(s["mixed"], j * units + (u + 1))
                    src = e[u % 3]
                    n = len(tiles)
                    for b in turn_parts(n, part):
                        at = next_turn()
                        for i in range(b, min(b + 4, n)):
                            last = pe.transpose(m.psum[:, at + (i - b) * P:at + (i - b + 1) * P],
                                                src[:, i * P:(i + 1) * P], m.ident[:, :])
                        last.then_inc(s["turned"], 1)
                    probs_at[u] = turn[0]

                probs_at = {}

                def values(u):
                    _, _, tiles = key_span(u)
                    pe.wait_ge(s["turn_read"], j * TURNS + probs_at[u])
                    at = next_bank(output=u)
                    col = (u % per_tile) * dv if l == 1 else 0
                    for i, kt in enumerate(tiles):
                        last = pe.matmul(m.psum[:, at:at + dv], pt[u % 2][:, i * P:(i + 1) * P],
                                         vt[:, kt, col:col + dv], start=(i == 0), stop=(i == len(tiles) - 1))
                    last.then_inc(s["pv_done"], 1)

                def turn_out():
                    if l == 0:
                        pe.wait_ge(s["o_read"], j * units + units)
                    for b in range(0, NT, 4):
                        if l == 1:
                            pe.wait_ge(s["o_normed"], j * 2 + (1 if b + 4 <= NORM_PARTS[0][1] else 2))
                        for p in range(2):
                            at = next_turn()
                            for t in range(b, min(b + 4, NT)):
                                last = pe.transpose(m.psum[:, at + (t - b) * P:at + (t - b + 1) * P],
                                                    o[:, t, p * P:(p + 1) * P], m.ident[:, :])
                            last.then_inc(s["turned"], 1)

                def stage_noted(qt):
                    stage(qt)
                    staged[qt] = turn[0]

                program(dict(cache_keys=cache_keys, project=project, turn_keys=turn_keys, stage=stage_noted,
                                        scores=scores, turn_probs=turn_probs, values=values, turn_out=turn_out))
                assert turn[0] == TURNS, (turn[0], TURNS)

        @block.scalar
        def _(act):
            with act.Fori(0, groups) as j:
                turn, used = [0], [0]

                def read_turn(out, width, scale=None, groups_of=None):
                    turn[0] += 1
                    used[0] += 1
                    act.wait_ge(s["turned"], j * TURNS + turn[0])
                    at = turn_bank(used[0] - 1)
                    src = m.psum[:, at:at + width]
                    if groups_of:
                        src = src.rearrange(groups_of[0], **groups_of[1])
                    if scale is None:
                        act.copy(out, src).then_inc(s["turn_read"], 1)
                    else:
                        act.activation(out, src, ACT.Copy, scale=scale).then_inc(s["turn_read"], 1)

                def turn_keys(i):
                    read_turn(ks[:, :, i * P:(i + 1) * P], nk * P, groups_of=("p (n t) -> p n t", dict(t=P)))

                def cache_keys():
                    for i in range(PT_TILES):
                        turn_keys(i)

                def split_tokens(t):
                    if t >= 2:
                        act.wait_ge((s["z_done"], s["v_done"])[l], j * NT + (t - 1))
                    act.copy(hs[t % 2][:, 0, :, :], h[:, :, t * P:(t + 1) * P]).then_inc(s["h_high"], 1)

                def split_weights():
                    act.wait_ge(s["w_loaded"], j * (16 * pre.pieces) + 16 * pre.pieces)
                    for k in range(KB):
                        act.copy(w_hi[:, k, :], w[:, k, :]).then_inc(s["w_high"], 1)

                def project(t):
                    if t == 0:
                        act.wait_ge(s["pv_done"], j * units)
                        split_tokens(0)
                        split_weights()
                    if t + 1 < NT:
                        split_tokens(t + 1)
                    z = m.psum[:, (t % 2) * BANK:(t % 2) * BANK + nz * HD]
                    act.wait_ge(s["z_done"], j * NT + (t + 1))
                    act.wait_ge(s["ssq"], j * NT + t)
                    act.activation(sq, z, ACT.Square).then_inc(s["squared"], 1)
                    v = m.psum[:, (t % 2) * BANK + nz * HD:(t % 2) * BANK + zw]
                    if l == 1:
                        act.wait_ge(s["v_done"], j * NT + (t + 1))
                        v = m.psum[:, (2 + t % 2) * BANK:(2 + t % 2) * BANK + vw]
                    if t == NT - 1:
                        act.wait_ge(s["k_stored"], j * 32)
                    act.copy(vt[:, PT_TILES + t, :], v).then_inc(s["v_copied"], 1)

                def stage(qt):
                    for half in range(2):
                        read_turn(qst[qt % 2][:, 2 * half:2 * half + 2, :, :].rearrange("p n v t -> p (n v) t"), 4 * P,
                                  groups_of=("p (n t) -> p n t", dict(t=P)))

                def scores(u, which):
                    if u <= 1:
                        exps(u, which)

                def exps(u, which):
                    lo, hi, _ = key_span(u)
                    for i in (which,):
                        n = u * maps + i
                        act.wait_ge(s["maxed"], j * nmaps + (n + 1))
                        out = e[3] if i == 1 else e[u % 3]
                        act.activation(out[:, 0:hi - lo], m.psum[:, score_at(n):score_at(n) + hi - lo], ACT.Exp,
                                       bias=neg_max[:, n:n + 1], accum_out=sums[:, n:n + 1]).then_inc(s["expd"], 1)

                def turn_probs(u, part):
                    _, _, tiles = key_span(u)
                    if u >= 2 and part == 0:
                        act.wait_ge(s["pv_done"], j * units + (u - 1))
                    for b in turn_parts(len(tiles), part):
                        n = min(4, len(tiles) - b)
                        read_turn(pt[u % 2][:, b * P:(b + n) * P], n * P)
                    if part < maps and u + 2 < units:
                        exps(u + 2, part)

                def values(u):
                    used[0] += 1
                    if l == 1 and u >= 1:
                        square_out(u - 1)

                def square_out(u):
                    act.wait_ge(s["o_read"], j * units + (u + 1))
                    act.activation(o_waste, o[:, u // per_tile, (u % per_tile) * dv:(u % per_tile + 1) * dv], ACT.Square,
                                   accum_out=osum[:, u:u + 1]).then_inc(s["o_squared"], 1)
                    act.drain()

                def turn_out():
                    if l == 1:
                        square_out(units - 1)
                        act.wait_ge(s["x_saved"], 16)
                    for b in range(0, NT, 4):
                        for p in range(2):
                            n = min(4, NT - b)
                            out = cat[:, ds(j * 2 + p, 1), b * P:(b + n) * P].rearrange("p o t -> p (o t)")
                            read_turn(out, n * P, scale=m.subln[:, 0:1] if l == 1 else None)

                program(dict(cache_keys=cache_keys, project=project, turn_keys=turn_keys, stage=stage,
                                        scores=scores, turn_probs=turn_probs, values=values, turn_out=turn_out))

        @block.vector
        def _(dve):
            dve.wait_ge(s["tables_loaded"], 96)
            dve.tensor_scalar(gains[:, 0, :], gains[:, 0, :], HD ** -0.5, None, ALU.mult)
            dve.drain()
            for tab in (cos_t, sin_t):
                for i in range(2):
                    dve.tensor_tensor(tab[:, :, i, :], tab[:, :, i, :],
                                      gains[:, i, :].unsqueeze(1).broadcast_to([P, LT, HD]), ALU.mult)
            dve.drain()
            with dve.Fori(0, groups) as j:
                def split_keys(i, src):
                    if i >= 2:
                        dve.wait_ge(s["turned"], j * TURNS + (i - 1))
                    view = src.rearrange("p (n d) -> p n d", d=HD)
                    dve.tensor_copy(khl[i % 2][:, :, 0, :].bitcast(F32R), view)
                    dve.drain()
                    dve.tensor_tensor(khl[i % 2][:, :, 1, :], view, khl[i % 2][:, :, 0, :], ALU.subtract
                                      ).then_inc(s["k_split"], 1)

                def cache_keys():
                    dve.wait_ge(s["cache_loaded"], j * (32 * PT_TILES) + 32 * PT_TILES)
                    for i in range(PT_TILES):
                        split_keys(i, kc[:, i, :])

                def split_tokens(t):
                    dve.wait_ge(s["h_high"], j * NT + (t + 1))
                    dve.tensor_tensor(hs[t % 2][:, 1, :, :], h[:, :, t * P:(t + 1) * P],
                                      hs[t % 2][:, 0, :, :].bitcast(F32), ALU.subtract).then_inc(s["h_split"], 1)

                def split_weights():
                    for k in range(KB):
                        dve.wait_ge(s["w_high"], j * KB + (k + 1))
                        dve.tensor_tensor(w_lo[:, k, :], w[:, k, :], w_hi[:, k, :].bitcast(F32), ALU.subtract
                                          ).then_inc(s["w_split"], 1)

                def project(t):
                    if 1 <= t < NT - 1:
                        split_tokens(t + 1)
                    z = m.psum[:, (t % 2) * BANK:(t % 2) * BANK + nz * HD]
                    parts = ((0, nq, 0), (nq, nz, 1))
                    dve.wait_ge((s["v_copied"], s["squared"])[l], j * NT + (t + 1))
                    dve.tensor_reduce(red[:, 0:nz], sq.rearrange("p (n d) -> p n d", d=HD), AX.X, ALU.add)
                    dve.drain()
                    dve.tensor_scalar(m.ssq[:, 0:nz], red[:, 0:nz], 1.0 / HD, EPS, ALU.mult, ALU.add).then_inc(s["ssq"], 1)
                    if t < LT:
                        for dst, tab in ((za, cos_t), (zb, sin_t)):
                            for lo, hi, i in parts:
                                last = dve.tensor_tensor(
                                    dst[:, lo * HD:hi * HD].rearrange("p (n d) -> p n d", d=HD),
                                    z[:, lo * HD:hi * HD].rearrange("p (n d) -> p n d", d=HD),
                                    tab[:, t, i, :].unsqueeze(1).broadcast_to([P, hi - lo, HD]), ALU.mult)
                        last.then_inc(s["z_read"], 1)
                        dve.drain()
                        halves = lambda b: b[:, :].rearrange("p (n h f) -> p n h f", h=2, f=16)
                        dve.tensor_tensor(halves(zc), halves(za), halves(zb)[:, :, ::-1, :], ALU.add)
                    else:
                        for lo, hi, i in parts:
                            last = dve.tensor_tensor(
                                zc[:, lo * HD:hi * HD].rearrange("p (n d) -> p n d", d=HD),
                                z[:, lo * HD:hi * HD].rearrange("p (n d) -> p n d", d=HD),
                                gains[:, i, :].unsqueeze(1).broadcast_to([P, hi - lo, HD]), ALU.mult)
                        last.then_inc(s["z_read"], 1)
                    dve.drain()
                    dve.wait_ge(s["rstd"], j * NT + (t + 1))
                    if t == NT - 1:
                        dve.wait_ge(s["k_stored"], j * 32)
                    for lo, hi, i in parts:
                        dst = (qtok[:, t, :], kf[:, :])[i].rearrange("p (n d) -> p n d", d=HD)
                        last = dve.tensor_tensor(dst, zc[:, lo * HD:hi * HD].rearrange("p (n d) -> p n d", d=HD),
                                                 m.rstd[:, lo:hi].unsqueeze(2).broadcast_to([P, hi - lo, HD]), ALU.mult)
                    if t == NT - 1:
                        last.then_inc(s["k_new"], 1)
                    dve.drain()
                    key_turns[0] = t
                    split_keys_at(t + PT_TILES)

                key_turns = [0]

                def split_keys_at(i):
                    split_keys(i, kf[:, :])
                    dve.drain()

                def split_queries(qt):
                    if qt >= 1:
                        dve.wait_ge(s["turned"], j * TURNS + staged_at[qt - 1])
                    view = qtok[:, qt, :].rearrange("p (n d) -> p n d", d=HD)
                    dve.tensor_copy(qq[:, :, 0, :].bitcast(F32R), view)
                    dve.tensor_copy(qq[:, :, 2, :].bitcast(F32R), view)
                    dve.drain()
                    dve.tensor_tensor(qq[:, :, 1, :], view, qq[:, :, 0, :], ALU.subtract).then_inc(s["q_split"], 1)

                staged_at, out_bank, count, used = {}, {}, [turns_k], [turns_k]

                def count_stage(qt):
                    count[0] += 2
                    used[0] += 2
                    staged_at[qt] = count[0]

                def count_probs(u, part):
                    count[0] += len(turn_parts(len(key_span(u)[2]), part))
                    used[0] += len(turn_parts(len(key_span(u)[2]), part))

                def count_values(u):
                    out_bank[u] = turn_bank(used[0])
                    used[0] += 1

                none = lambda *_: None
                program(dict(cache_keys=none, project=none, turn_keys=none, stage=count_stage, scores=none,
                                        turn_probs=count_probs, values=count_values, turn_out=none))

                def maxima(u, which):
                    lo, hi, _ = key_span(u)
                    for i in (which,):
                        n = u * maps + i
                        dve.wait_ge(s["scored"], j * nmaps + (n + 1))
                        dve.tensor_reduce(neg_max[:, n:n + 1], m.psum[:, score_at(n):score_at(n) + hi - lo], AX.X,
                                          ALU.max, negate=True).then_inc(s["maxed"], 1)

                def mix(u):
                    n = u * maps
                    dve.wait_ge(s["expd"], j * nmaps + (n + maps))
                    dve.reciprocal(inv[:, n:n + maps], sums[:, n:n + maps])
                    if l == 1:
                        lo, hi, _ = key_span(u)
                        dve.drain()
                        dve.tensor_scalar(ratio[:, u:u + 1], sums[:, n:n + 1], inv[:, n + 1:n + 2], m.neg_lambda[:, 0:1],
                                          ALU.mult, ALU.mult)
                        dve.drain()
                        probs = e[u % 3][:, 0:hi - lo]
                        dve.scalar_tensor_tensor(probs, e[3][:, 0:hi - lo], ratio[:, u:u + 1], probs, ALU.mult, ALU.add
                                                 ).then_inc(s["mixed"], 1)

                def read_out(u):
                    at = out_bank[u]
                    if l == 0:
                        dve.drain()
                    dve.wait_ge(s["pv_done"], j * units + (u + 1))
                    c = (u % per_tile) * dv
                    dve.tensor_scalar(o[:, u // per_tile, c:c + dv], m.psum[:, at:at + dv],
                                      inv[:, u * maps:u * maps + 1], None, ALU.mult).then_inc(s["o_read"], 1)

                heads = lambda b: b[:, :, :].rearrange("p t (n d) -> p (t n) d", d=dv)

                def norm_mean(i):
                    lo, hi = (2 * t for t in NORM_PARTS[i])
                    dve.wait_ge(s["o_squared"], j * units + hi)
                    dve.tensor_scalar(m.ssq[:, lo:hi], osum[:, lo:hi], 1.0 / dv, EPS, ALU.mult, ALU.add
                                      ).then_inc(s["o_mean"], 1)

                def norm_out(i):
                    lo, hi = (2 * t for t in NORM_PARTS[i])
                    dve.wait_ge(s["o_rstd"], j * 2 + (i + 1))
                    dve.tensor_tensor(heads(o)[:, lo:hi, :], heads(o)[:, lo:hi, :],
                                      m.rstd[:, lo:hi].unsqueeze(2).broadcast_to([P, hi - lo, dv]), ALU.mult
                                      ).then_inc(s["o_normed"], 1)

                split_tokens(0)
                split_weights()
                split_tokens(1)
                cache_keys()
                for t in range(NT):
                    project(t)
                split_queries(0)
                for i in range(maps):
                    maxima(0, i)
                for u in range(units + 2):
                    if u % per_tile == 0 and u // per_tile + 1 < NT:
                        split_queries(u // per_tile + 1)
                    if u + 1 < units:
                        maxima(u + 1, 0)
                    if u < units:
                        mix(u)
                    if u + 1 < units and maps == 2:
                        maxima(u + 1, 1)
                    if l == 1 and u == units - 1:
                        norm_mean(0)
                    if l == 1 and u == units + 1:
                        norm_out(0)
                    if u >= 2:
                        read_out(u - 2)
                dve.drain()
                if l == 1:
                    norm_mean(1)
                    norm_out(1)
                    dve.drain()


def out_weights(nc, m, a, sem, l):
    pre = Memory()
    put = placer(m, f"out{l}", m.scratch_at, m.end)
    pre.w = [put(f"w{i}", [P, KB, P]) for i in range(2)]
    pre.end = put.pos[0]
    pre.loaded = [sem(f"o{l}_loaded{i}") for i in range(2)]
    pre.src = (a["l0_w_out"], a["l1_w_out"])[l].rearrange("(k p) n -> p k n", p=P)

    def ahead(sp):
        for i in range(2):
            sp.dma_start(pre.w[i][:, :, :], pre.src[:, :, i * P:(i + 1) * P]).then_inc(pre.loaded[i], 16)

    pre.ahead = ahead
    return pre


THIRD = TOK // 3


def out_projection(nc, m, a, sem, l, x, cat, pre):
    w, w_out = pre.w, pre.src
    put = placer(m, f"outs{l}", pre.end, m.end)
    w_hi, w_lo = ([put(f"{n}{i}", [P, KB, P], F32R) for i in range(2)] for n in ("w_hi", "w_lo"))
    cat_hi = put("cat_hi", [P, KB, TOK], F32R)
    cat_lo = m.tensor(f"outs{l}_cat_lo", [P, KB, TOK], F32R, m.region_at[l])
    loaded = pre.loaded
    done, added, w_high, w_split = ([sem(f"o{l}_{n}{i}") for i in range(2)] for n in ("done", "added", "w_high", "w_split"))
    cat_high, cat_split = (sem(f"o{l}_" + n) for n in ("cat_high", "cat_split"))
    pieces = [(c, lo, hi, cond) for c in range(3) for lo, hi, cond in
              (((0, THIRD, 0),) if c < 2 else ((0, LAT - 2 * THIRD, 0), (LAT - 2 * THIRD, THIRD, 1)))]
    with nc.Block() as block:
        @block.sync
        def _(sp):
            with sp.Fori(0, KB // 2 - 1) as r:
                for i in range(2):
                    wait_value(m, sp, w_split[i], r + 1)
                    sp.dma_start(w[i][:, :, :], w_out[:, :, ds(r * 2 * P + (2 + i) * P, P)]).then_inc(loaded[i], 16)

        @block.tensor
        def _(pe):
            with pe.Fori(0, KB // 2) as r:
                for i in range(2):
                    pe.wait_ge(w_split[i], r + 1)
                    pe.wait_ge(added[i], r)
                    for k in range(KB):
                        if i == 0:
                            pe.wait_ge(cat_split, k + 1)
                        for n, (lhs, rhs) in enumerate(((w_hi, cat_hi), (w_hi, cat_lo), (w_lo, cat_hi))):
                            for c in range(3):
                                at = (i * 3 + c) * BANK
                                right = rhs[:, k, c * THIRD:(c + 1) * THIRD]
                                last = pe.matmul(m.psum[:, at:at + THIRD], lhs[i][:, k, :],
                                                 right,
                                                 start=(k == 0 and n == 0), stop=(k == KB - 1 and n == 2))
                    last.then_inc(done[i], 1)

        @block.scalar
        def _(act):
            def split(r, i):
                act.wait_ge(loaded[i], r * 16 + 16)
                act.wait_ge(done[i], r)
                act.copy(w_hi[i][:, :, :], w[i][:, :, :]).then_inc(w_high[i], 1)

            for i in range(2):
                split(0, i)
                if i == 0:
                    for k in range(KB):
                        act.copy(cat_hi[:, k, :], cat[:, k, :]).then_inc(cat_high, 1)
            with act.Fori(1, KB // 2) as r:
                for i in range(2):
                    split(r, i)

        @block.vector
        def _(dve):
            def split(r, i):
                dve.wait_ge(w_high[i], r + 1)
                dve.tensor_tensor(w_lo[i][:, :, :], w[i][:, :, :], w_hi[i][:, :, :].bitcast(F32), ALU.subtract
                                  ).then_inc(w_split[i], 1)

            for i in range(2):
                split(0, i)
                if i == 0:
                    for k in range(KB):
                        dve.wait_ge(cat_high, k + 1)
                        dve.tensor_tensor(cat_lo[:, k, :], cat[:, k, :], cat_hi[:, k, :].bitcast(F32),
                                          ALU.subtract).then_inc(cat_split, 1)

            def add(r, i):
                dve.wait_ge(done[i], r + 1)
                for c, lo, hi, cond in pieces:
                    xs = x[:, ds(r * 2 + i, 1), c * THIRD + lo:c * THIRD + hi].rearrange("p o t -> p (o t)")
                    gate = m.mod[l][:, ds(r * 2 + (2 * KB + i), 1), cond:cond + 1].rearrange("p o c -> p (o c)")
                    at = (i * 3 + c) * BANK
                    last = dve.scalar_tensor_tensor(xs, m.psum[:, at + lo:at + hi], gate, xs, ALU.mult, ALU.add)
                last.then_inc(added[i], 1)

            with dve.Fori(0, KB // 2 - 1) as r:
                for i in range(2):
                    add(r, i)
                    split(r + 1, i)
            with dve.Fori(KB // 2 - 1, KB // 2) as r:
                for i in range(2):
                    add(r, i)


def moe_memory(m, a, sem, l, h_at):
    put = placer(m, f"moe{l}", m.scratch_at, m.end)
    mm = Memory()
    mm.w = [put(f"w{i}", [P, KB, BANK]) for i in range(6)]
    mm.h_ctx = m.tensor(f"moe{l}_h_ctx", [P, D], F32, put.pos[0])
    mm.x_next = put("x_next", [P, D])
    mm.idx = put("idx", [P, 20], U32)
    mm.gate = put("gate", [P, EXP])
    mm.idx_now = put("idx_now", [P, 2], U32)
    mm.sel_gate = put("sel_gate", [P, 2, P])
    mm.x_ctx = put("x_ctx", [P, KB, 2 * P + 16])
    mm.act = [put(f"act{i}", [P, ROWS]) for i in range(2)]
    mm.iota = put("iota", [P, P])
    mm.small = put("small", [P, 64])
    mm.spare_at = put.pos[0]
    mm.loaded = [sem(f"e{l}_loaded{i}") for i in range(6)]
    wg, wu, wd = ((a["l0_w_gate"], a["l0_w_up"], a["l0_w_down"]), (a["l1_w_gate"], a["l1_w_up"], a["l1_w_down"]))[l]
    slot_src = ((wg, 0), (wu, 0), (wg, 1), (wu, 1), (wd, 0), (wd, 1))

    def load(sp, i, e):
        w, half = slot_src[i]
        src = w[ds(e, 1)].rearrange("o r n -> (o r) n").rearrange("(k p) n -> p k n", p=P)
        sp.dma_start(mm.w[i][:, :, :], src[:, :, half * BANK:(half + 1) * BANK]).then_inc(mm.loaded[i], 16)

    mm.load = load
    put = placer(m, f"moeh{l}", h_at, h_at + KB * TOK * 4)
    mm.xe = put("xe", [P, KB, ROWS])
    mm.hid = put("hid", [P, KB, ROWS])
    mm.yt = put("yt", [P, KB, CAP_L])
    mm.ye = put("ye", [P, D])
    mm.y_ctx = put("y_ctx", [P, KB, 2 * P])
    mm.ye_ctx = put("ye_ctx", [P, 2, D // 2])
    return mm


def routing(nc, m, a, sem, l, h, mm, dram, ada=None):
    slots_end = m.scratch_at + 6 * 16384
    put = placer(m, f"route{l}", slots_end - 35328, slots_end)
    router = put("router", [P, KB, EXP])
    stage = [put(f"stage{i}", [P, D]) for i in range(4)]
    zeros = put("zeros", [P, D])
    logits = put("logits", [P, NT, EXP])
    red = put("red", [P, 2, NT])
    aff = put("aff", [EXP, 2, TOK])
    top = put("top", [EXP, CAP_L + CAP_C])
    topi = put("topi", [EXP, CAP_L + CAP_C], U32)
    topf = put("topf", [EXP, CAP_L + CAP_C])
    pair = put("pair", [P, 2, 2])
    sel01 = put("sel01", [P, 2, P])
    sel_t = put("sel_t", [P, 2 * P])
    iota_i = put("iota_i", [P, P], I32)
    names = ("router_loaded", "zeroed", "zero_stored", "scored", "maxed", "expd", "soft", "aff_turned",
             "aff_ready", "turned", "turn_read", "topped", "top_turned", "pair_out", "pair_in", "sel_ready",
             "sel_turned", "sel_copied", "ctx_done", "iota_ready")
    s = {n: sem(f"r{l}_" + n) for n in names}
    stored = [sem(f"r{l}_stored{i}") for i in range(4)]
    score_ps = m.psum[:, 4 * BANK:4 * BANK + NT * EXP]
    batches = [(t, half) for t in range(NT) for half in range(2)]

    with nc.Block() as block:
        @block.sync
        def _(sp):
            r = (a["l0_router"], a["l1_router"])[l].rearrange("(k p) e -> p k e", p=P)
            sp.dma_start(router[:, :, :], r).then_inc(s["router_loaded"], 16)
            if ada:
                ada.ahead(sp)
            for i in range(2):
                mm.load(sp, i, 0)
            sp.wait_ge(s["zeroed"], 1)
            for t in range(LT):
                sp.dma_start(dram["y"][t * P:(t + 1) * P, :], zeros[:, :]).then_inc(s["zero_stored"], 16)
            for t in range(LT):
                sp.wait_ge(s["turn_read"], 2 * t + 2)
                sp.dma_start(dram["h"][t * P:(t + 1) * P, :], stage[t % 4][:, :]).then_inc(stored[t % 4], 16)
            if ada:
                ada.loads(sp)
            sp.wait_ge(s["topped"], 2)
            sp.dma_start(dram["pair"][0], topf[:, CAP_L:]).then_inc(s["pair_out"], 16)
            sp.dma_start(dram["pair"][1], top[:, CAP_L:]).then_inc(s["pair_out"], 16)
            sp.wait_ge(s["pair_out"], 32)
            for i in range(2):
                sp.dma_start(pair[:, i, :], dram["pair"][i].rearrange("e c -> (e c)").rearrange("(p j) -> p j", j=2)
                             ).then_inc(s["pair_in"], 16)
            for q in stored:
                sp.wait_ge(q, 16 * LT // 4)
            sp.wait_ge(s["zero_stored"], 16 * LT)

        @block.gpsimd
        def _(pool):
            pool.iota(iota_i[:, :], [[1, P]], base=0, channel_multiplier=0).then_inc(s["iota_ready"], 1)
            pool.memset(zeros[:, :], 0.0).then_inc(s["zeroed"], 1)

        @block.tensor
        def _(pe):
            pe.wait_ge(s["router_loaded"], 16)
            for t in range(NT):
                for k in range(KB):
                    last = pe.matmul(score_ps[:, t * EXP:(t + 1) * EXP], h[:, k, t * P:(t + 1) * P], router[:, k, :],
                                     start=(k == 0), stop=(k == KB - 1))
            last.then_inc(s["scored"], 1)

            def turn(i):
                t, half = batches[i]
                if i >= 4:
                    pe.wait_ge(s["turn_read"], i - 3)
                for k in range(4):
                    last = pe.transpose(m.psum[:, (i % 4) * BANK + k * P:(i % 4) * BANK + (k + 1) * P],
                                        h[:, 4 * half + k, t * P:(t + 1) * P], m.ident[:, :])
                last.then_inc(s["turned"], 1)

            for i in range(4):
                turn(i)
            pe.wait_ge(s["soft"], 1)
            for t in range(NT):
                last = pe.transpose(m.psum[0:EXP, 5 * BANK + t * P:5 * BANK + (t + 1) * P], logits[:, t, :], m.ident[:, :])
            last.then_inc(s["aff_turned"], 1)
            for i in range(4, len(batches)):
                turn(i)
            if ada:
                pe.wait_ge(s["aff_ready"], 1)
                ada.products(pe)
            pe.wait_ge(s["topped"], 3)
            pe.transpose(m.psum[:, 4 * BANK:4 * BANK + EXP], topf[:, 0:CAP_L], m.ident[0:EXP, 0:EXP])
            pe.transpose(m.psum[:, 4 * BANK + EXP:4 * BANK + 2 * EXP], top[:, 0:CAP_L], m.ident[0:EXP, 0:EXP]
                         ).then_inc(s["top_turned"], 1)
            pe.wait_ge(s["sel_ready"], 1)
            for i in range(2):
                last = pe.transpose(m.psum[:, 5 * BANK + i * P:5 * BANK + (i + 1) * P], sel01[:, i, :], m.ident[:, :])
            last.then_inc(s["sel_turned"], 1)
            pe.wait_ge(s["sel_copied"], 1)
            pe.wait_ge(s["turn_read"], len(batches))
            for k in range(KB):
                last = pe.matmul(m.psum[:, k * 2 * P:(k + 1) * 2 * P], mm.h_ctx[:, k * P:(k + 1) * P], sel_t[:, :],
                                 start=True, stop=True)
            last.then_inc(s["ctx_done"], 1)

        @block.scalar
        def _(act):
            act.wait_ge(s["maxed"], 1)
            act.activation(logits[:, :, :], logits[:, :, :], ACT.Exp).then_inc(s["expd"], 1)
            for i, (t, half) in enumerate(batches):
                if t >= 4 and half == 0 and t < LT:
                    act.wait_ge(stored[t % 4], 16 * (t // 4))
                act.wait_ge(s["turned"], i + 1)
                dst = stage[t % 4] if t < LT else mm.h_ctx
                act.copy(dst[:, half * BANK:(half + 1) * BANK], m.psum[:, (i % 4) * BANK:(i % 4 + 1) * BANK]
                         ).then_inc(s["turn_read"], 1)
            if ada:
                ada.copies(act)
            act.wait_ge(s["ctx_done"], 1)
            act.copy(mm.x_ctx[:, :, 0:2 * P], m.psum[:, 0:KB * 2 * P].rearrange("p (k c) -> p k c", k=KB))

        @block.vector
        def _(dve):
            dve.wait_ge(s["iota_ready"], 1)
            dve.tensor_copy(mm.iota[:, :], iota_i[:, :])
            dve.memset(mm.x_ctx[:, :, 2 * P:], 0.0)
            dve.wait_ge(s["scored"], 1)
            scores = score_ps.rearrange("p (t e) -> p t e", e=EXP)
            wide = lambda v: v.unsqueeze(2).broadcast_to([P, NT, EXP])
            dve.tensor_reduce(red[:, 0, :], scores, AX.X, ALU.max)
            dve.drain()
            dve.tensor_tensor(logits[:, :, :], scores, wide(red[:, 0, :]), ALU.subtract).then_inc(s["maxed"], 1)
            dve.wait_ge(s["expd"], 1)
            dve.tensor_reduce(red[:, 1, :], logits[:, :, :], AX.X, ALU.add)
            dve.drain()
            dve.reciprocal(red[:, 0, :], red[:, 1, :])
            dve.drain()
            dve.tensor_tensor(logits[:, :, :], logits[:, :, :], wide(red[:, 0, :]), ALU.mult).then_inc(s["soft"], 1)
            dve.wait_ge(s["aff_turned"], 1)
            dve.tensor_copy(aff[:, 0, :], m.psum[0:EXP, 5 * BANK:5 * BANK + TOK]).then_inc(s["aff_ready"], 1)
            dve.drain()

            def choose(lo, hi, n, at):
                cur = aff[:, 0, lo:hi]
                for r in range(n // 8):
                    v, ix = top[:, at + 8 * r:at + 8 * r + 8], topi[:, at + 8 * r:at + 8 * r + 8]
                    dve.max(v, cur)
                    dve.drain()
                    last = dve.max_index(ix, v, cur)
                    if r + 1 < n // 8:
                        nxt = aff[:, (r + 1) % 2, lo:hi]
                        dve.match_replace(nxt, v, cur, -1.0)
                        dve.drain()
                        cur = nxt
                dve.drain()
                return dve.tensor_copy(topf[:, at:at + n], topi[:, at:at + n])

            choose(LAT, TOK, CAP_C, CAP_L).then_inc(s["topped"], 1)
            dve.drain()
            dve.sem_inc(s["topped"], 1)
            choose(0, LAT, CAP_L, 0).then_inc(s["topped"], 1)
            if ada:
                ada.vectors(dve)
            dve.wait_ge(s["pair_in"], 32)
            for i in range(2):
                dve.tensor_scalar(sel01[:, i, :], mm.iota[:, :], pair[:, 0, i:i + 1], None, ALU.is_equal)
                last = dve.tensor_scalar(mm.sel_gate[:, i, :], mm.iota[:, :], pair[:, 0, i:i + 1], pair[:, 1, i:i + 1],
                                         ALU.is_equal, ALU.mult)
            last.then_inc(s["sel_ready"], 1)
            dve.wait_ge(s["top_turned"], 1)
            dve.tensor_copy(mm.idx[:, 0:EXP], m.psum[:, 4 * BANK:4 * BANK + EXP])
            dve.tensor_copy(mm.idx[:, EXP:EXP + 1], m.psum[:, 4 * BANK:4 * BANK + 1])
            dve.tensor_copy(mm.gate[:, :], m.psum[:, 4 * BANK + EXP:4 * BANK + 2 * EXP])
            dve.wait_ge(s["sel_turned"], 1)
            dve.tensor_copy(sel_t[:, :], m.psum[:, 5 * BANK:5 * BANK + 2 * P]).then_inc(s["sel_copied"], 1)


def experts(nc, m, a, sem, l, x, mm, dram):
    names = ("quarter", "rows_in", "idx_set", "gathered", "x_turned", "x_read", "pair_done", "silu_done",
             "hid_done", "down_done", "down_read", "y_turned", "y_read", "scattered", "ctx_turned",
             "ctx_copied", "ctx_done")
    s = {n: sem(f"e{l}_" + n) for n in names}
    loaded = mm.loaded
    FB = KB

    with nc.Block() as block:
        @block.sync
        def _(sp):
            sp.wait_ge(s["gathered"], 16)
            for i in range(2, 6):
                mm.load(sp, i, 0)
            with sp.Fori(0, EXP - 1) as e:
                for q, slots in enumerate(((0, 1), (2, 3), (4,), (5,))):
                    wait_value(m, sp, s["quarter"], e * 4 + (q + 1))
                    for i in slots:
                        mm.load(sp, i, e + 1)

        @block.gpsimd
        def _(pool):
            def gather():
                pool.indirect_dma_start(mm.x_next[:, :], None, dram["h"], bass.IndirectOffsetOnAxis(ap=mm.idx_now[:, 0:1], axis=0)
                                        ).then_inc(s["gathered"], 16)

            pool.wait_ge(s["idx_set"], 1)
            gather()
            with pool.Fori(0, EXP) as e:
                wait_value(m, pool, s["idx_set"], e + 2)
                gather()
                wait_value(m, pool, s["y_read"], e * 2 + 2)
                wait_value(m, pool, s["scattered"], e * 16)
                pool.indirect_dma_start(dram["y"], bass.IndirectOffsetOnAxis(ap=mm.idx_now[:, 1:2], axis=0), mm.ye[:, :], None,
                                        compute_op=ALU.add).then_inc(s["scattered"], 16)
            pool.wait_ge(s["scattered"], 16 * EXP)
            pool.wait_ge(s["gathered"], 16 * (EXP + 1))

        @block.tensor
        def _(pe):
            def turn_rows(done):
                for k in range(KB):
                    last = pe.transpose(m.psum[:, 2 * BANK + k * P:2 * BANK + (k + 1) * P],
                                        mm.x_next[:, k * P:(k + 1) * P], m.ident[:, :])
                last.then_inc(s["x_turned"], 1)

            pe.wait_ge(s["gathered"], 16)
            turn_rows(0)
            with pe.Fori(0, EXP) as e:
                pe.wait_ge(s["x_read"], e + 1)
                for f in range(FB):
                    if f % 4 == 0:
                        for i in (2 * (f // 4), 2 * (f // 4) + 1):
                            pe.wait_ge(loaded[i], e * 16 + 16)
                    if f >= 2:
                        pe.wait_ge(s["hid_done"], e * FB + (f - 1))
                    col = (f % 4) * P
                    for i in range(2):
                        at = (f % 2) * BANK + i * ROWS
                        for k in range(KB):
                            last = pe.matmul(m.psum[:, at:at + ROWS], mm.w[2 * (f // 4) + i][:, k, col:col + P],
                                             mm.xe[:, k, :], start=(k == 0), stop=(k == KB - 1))
                    last.then_inc(s["pair_done"], 1)
                    if f % 4 == 3:
                        pe.wait_ge(s["pair_done"], e * FB + (f + 1))
                        pe.sem_inc(s["quarter"], 1)
                pe.wait_ge(s["gathered"], e * 16 + 32)
                turn_rows(e + 1)
                pe.wait_ge(s["hid_done"], e * FB + FB)

                def turn_y(n):
                    pe.wait_ge(s["down_read"], e * KB + (n + 1))
                    last = pe.transpose(m.psum[:, 6 * BANK + n * P:6 * BANK + (n + 1) * P], mm.yt[:, n, :], m.ident[:, :])
                    if n % 4 == 3:
                        last.then_inc(s["y_turned"], 1)

                for n in range(KB):
                    if n == 1:
                        pe.wait_ge(s["y_read"], e * 2)
                    if n % 4 == 0:
                        pe.wait_ge(loaded[4 + n // 4], e * 16 + 16)
                    if n >= 2:
                        pe.wait_ge(s["down_read"], e * KB + (n - 1))
                    at = (4 + n % 2) * BANK
                    for f in range(FB):
                        last = pe.matmul(m.psum[:, at:at + ROWS], mm.w[4 + n // 4][:, f, (n % 4) * P:(n % 4 + 1) * P],
                                         mm.hid[:, f, :], start=(f == 0), stop=(f == FB - 1))
                    last.then_inc(s["down_done"], 1)
                    if n % 4 == 3:
                        pe.wait_ge(s["down_done"], e * KB + (n + 1))
                        pe.sem_inc(s["quarter"], 1)
                    if n >= 1:
                        turn_y(n - 1)
                turn_y(KB - 1)
            for half in range(2):
                for i in range(2):
                    for n in range(4):
                        at = i * BANK + n * P
                        last = pe.transpose(m.psum[:, at:at + P], mm.y_ctx[:, 4 * half + n, i * P:(i + 1) * P], m.ident[:, :])
                last.then_inc(s["ctx_turned"], 1)
                pe.wait_ge(s["ctx_copied"], half + 1)
                for n in range(4):
                    for i in range(2):
                        last = pe.matmul(m.psum[:, (2 + half) * BANK + n * P:(2 + half) * BANK + (n + 1) * P],
                                         mm.ye_ctx[:, i, n * P:(n + 1) * P], mm.sel_gate[:, i, :],
                                         start=(i == 0), stop=(i == 1))
                last.then_inc(s["ctx_done"], 1)

        @block.scalar
        def _(act):
            def read_rows():
                act.copy(mm.xe[:, :, 0:CAP_L], m.psum[:, 2 * BANK:4 * BANK].rearrange("p (k c) -> p k c", k=KB)
                         ).then_inc(s["rows_in"], 1)

            act.wait_ge(s["x_turned"], 1)
            read_rows()
            with act.Fori(0, EXP) as e:
                for f in range(FB):
                    act.wait_ge(s["pair_done"], e * FB + (f + 1))
                    if f >= 2:
                        act.wait_ge(s["hid_done"], e * FB + (f - 1))
                    at = (f % 2) * BANK
                    act.activation(mm.act[f % 2][:, :], m.psum[:, at:at + ROWS], ACT.Silu).then_inc(s["silu_done"], 1)
                act.wait_ge(s["x_turned"], e + 2)
                read_rows()
                for n in range(KB):
                    act.wait_ge(s["down_done"], e * KB + (n + 1))
                    at = (4 + n % 2) * BANK
                    act.copy(mm.yt[:, n, :], m.psum[:, at:at + CAP_L])
                    dst = mm.y_ctx[:, n, :].rearrange("p (j r) -> p j r", j=2)[:, :, ds(e * 8, 8)]
                    act.copy(dst, m.psum[:, at + CAP_L:at + ROWS].rearrange("p (j r) -> p j r", j=2)
                             ).then_inc(s["down_read"], 1)

        @block.vector
        def _(dve):
            dve.tensor_copy(mm.idx_now[:, 0:1], mm.idx[:, 0:1]).then_inc(s["idx_set"], 1)
            ctx_rows = lambda e: mm.x_ctx[:, :, 0:2 * P].rearrange("p k (j r) -> p k j r", j=2)[:, :, :, ds(e * 8, 8)]
            dst = mm.xe[:, :, CAP_L:ROWS].rearrange("p k (j r) -> p k j r", j=2)
            for j in range(2):
                dve.tensor_copy(dst[:, :, j, :], mm.x_ctx[:, :, j * P:j * P + 8])
            dve.wait_ge(s["rows_in"], 1)
            dve.drain()
            dve.sem_inc(s["x_read"], 1)
            with dve.Fori(0, EXP) as e:
                for f in range(FB):
                    if f == 3:
                        dve.wait_ge(s["gathered"], e * 16 + 16)
                        dve.wait_ge(s["x_turned"], e + 1)
                        dve.wait_ge(s["scattered"], e * 16)
                        dve.tensor_copy(mm.idx_now[:, 1:2], mm.idx[:, ds(e, 1)])
                        dve.tensor_copy(mm.idx_now[:, 0:1], mm.idx[:, ds(e + 1, 1)]).then_inc(s["idx_set"], 1)
                    dve.wait_ge(s["silu_done"], e * FB + (f + 1))
                    at = (f % 2) * BANK + ROWS
                    dve.tensor_tensor(mm.hid[:, f, :], mm.act[f % 2][:, :], m.psum[:, at:at + ROWS], ALU.mult
                                      ).then_inc(s["hid_done"], 1)
                dve.wait_ge(s["x_turned"], e + 2)
                for j in range(2):
                    dve.tensor_copy(dst[:, :, j, :], mm.x_ctx[:, :, ds(e * 8 + (j * P + 8), 8)])
                dve.drain()
                dve.wait_ge(s["rows_in"], e + 2)
                dve.sem_inc(s["x_read"], 1)
                for half in range(2):
                    dve.wait_ge(s["y_turned"], e * 2 + (half + 1))
                    if half == 0:
                        dve.wait_ge(s["scattered"], e * 16)
                    at = (6 + half) * BANK
                    dve.tensor_scalar(mm.ye[:, half * BANK:(half + 1) * BANK], m.psum[:, at:at + BANK],
                                      mm.gate[:, ds(e, 1)], None, ALU.mult).then_inc(s["y_read"], 1)
            for half in range(2):
                dve.wait_ge(s["ctx_turned"], half + 1)
                if half == 1:
                    dve.wait_ge(s["ctx_done"], 1)
                dve.tensor_copy(mm.ye_ctx[:, :, :], m.psum[:, 0:2 * BANK].rearrange("p (i n) -> p i n", i=2)
                                ).then_inc(s["ctx_copied"], 1)
            for half in range(2):
                dve.wait_ge(s["ctx_done"], half + 1)
                for n in range(4):
                    k = 4 * half + n
                    xs = x[:, k, LAT:TOK]
                    dve.scalar_tensor_tensor(xs, m.psum[:, (2 + half) * BANK + n * P:(2 + half) * BANK + (n + 1) * P],
                                             m.mod[l][:, 5 * KB + k, 1:2], xs, ALU.mult, ALU.add)


def add_experts(nc, m, a, sem, l, x, y_at, dram):
    put = placer(m, f"add{l}", y_at, y_at + KB * TOK * 4)
    y = put("y", [P, LT, D])
    put = placer(m, f"addo{l}", m.scratch_at, m.end)
    out = [put(f"out{i}", [P, D]) for i in range(4)]
    loaded = [sem(f"add{l}_loaded{t}") for t in range(LT)]
    turned, added, out_turned, out_read = (sem(f"add{l}_" + n) for n in ("turned", "added", "out_turned", "out_read"))
    stored = [sem(f"add{l}_stored{i}") for i in range(4 * l)]
    out_tiles = [LT] + list(range(LT))
    with nc.Block() as block:
        @block.sync
        def _(sp):
            for t in range(LT):
                sp.dma_start(y[:, t, :], dram["y"][t * P:(t + 1) * P, :]).then_inc(loaded[t], 16)
            if l == 1:
                for n, t in enumerate(out_tiles):
                    sp.wait_ge(out_read, 2 * n + 2)
                    dst = a["y_sample"][0, t * P:(t + 1) * P, :] if t < LT else a["y_prompt"][0]
                    sp.dma_start(dst, out[n % 4][:, :]).then_inc(stored[n % 4], 16)
                for i in range(4):
                    sp.wait_ge(stored[i], 16 * len(range(i, NT, 4)))

        @block.tensor
        def _(pe):
            def turn_sum(t, half):
                i = 2 * t + half
                if i >= 4:
                    pe.wait_ge(added, i - 3)
                for k in range(4):
                    c = (4 * half + k) * P
                    last = pe.transpose(m.psum[:, (i % 4) * BANK + k * P:(i % 4) * BANK + (k + 1) * P],
                                        y[:, t, c:c + P], m.ident[:, :])
                last.then_inc(turned, 1)

            def turn_out(n):
                t = out_tiles[n]
                for half in range(2):
                    i = 2 * n + half
                    if t < LT:
                        pe.wait_ge(added, 2 * t + half + 1)
                    if i >= 4:
                        pe.wait_ge(out_read, i - 3)
                    for k in range(4):
                        at = (4 + i % 4) * BANK + k * P
                        last = pe.transpose(m.psum[:, at:at + P], x[:, 4 * half + k, t * P:(t + 1) * P], m.ident[:, :])
                    last.then_inc(out_turned, 1)

            for t in range(LT):
                if l == 1:
                    if t != 1:
                        turn_out(max(t - 1, 0))
                pe.wait_ge(loaded[t], 16)
                for half in range(2):
                    turn_sum(t, half)
            if l == 1:
                turn_out(LT - 1)
                turn_out(LT)

        @block.vector
        def _(dve):
            for t in range(LT):
                for half in range(2):
                    i = 2 * t + half
                    dve.wait_ge(turned, i + 1)
                    for k in range(4):
                        xs = x[:, 4 * half + k, t * P:(t + 1) * P]
                        last = dve.scalar_tensor_tensor(xs, m.psum[:, (i % 4) * BANK + k * P:(i % 4) * BANK + (k + 1) * P],
                                                        m.mod[l][:, 5 * KB + 4 * half + k, 0:1], xs, ALU.mult, ALU.add)
                    last.then_inc(added, 1)

        if l == 1:
            @block.scalar
            def _(act):
                for i in range(2 * NT):
                    n, half = i // 2, i % 2
                    if n >= 4 and half == 0:
                        act.wait_ge(stored[n % 4], 16 * (n // 4))
                    act.wait_ge(out_turned, i + 1)
                    at = (4 + i % 4) * BANK
                    act.copy(out[n % 4][:, half * BANK:(half + 1) * BANK], m.psum[:, at:at + BANK]).then_inc(out_read, 1)


def end_stage(nc, semaphores):
    nc.clear_and_free_semaphores(semaphores)
    semaphores.clear()
    nc.all_engine_barrier()


def build(nc, a):
    ctx = ExitStack()
    with ctx:
        m = memory(nc, ctx)
        m.passed = {nc.sync.engine: ctx.enter_context(nc.semaphore("sync_passed")),
                    nc.gpsimd.engine: ctx.enter_context(nc.semaphore("pool_passed"))}
        of_stage = []

        def sem(name):
            of_stage.append(nc.alloc_semaphore(name=name))
            return of_stage[-1]

        x_dram = nc.dram_tensor("x_saved_dram", [P, KB * TOK], F32, kind="Internal").ap()
        drams = [dict(h=nc.dram_tensor(f"h_rows{l}", [LAT, D], F32, kind="Internal").ap(),
                      y=nc.dram_tensor(f"y_rows{l}", [LAT, D], F32, kind="Internal").ap(),
                      pair=nc.dram_tensor(f"pairs{l}", [2, EXP, CAP_C], F32, kind="Internal").ap())
                 for l in range(2)]
        keep_sem = lambda name: ctx.enter_context(nc.semaphore(name))
        recurrent_pre = recurrent_weights(nc, m, a, keep_sem)
        attn_pre = [attention_weights(nc, m, a, keep_sem, l) for l in range(2)]
        out_pre = [out_weights(nc, m, a, keep_sem, l) for l in range(2)]
        shared = (nc, m, a, sem)
        end = lambda: end_stage(nc, of_stage)
        put = placer(m, "ada0", m.scratch_at, m.end)
        slots = [put(f"w{i}", [P, KB // 2, BANK]) for i in range(8)]
        rows = [put(f"row{i}", [2, BANK]) for i in range(2)]
        ada = adaln(m, a, keep_sem, 0, slots, rows, (0, 1), 2 * BANK)
        setup(*shared, ada.ahead)
        end()
        modulation(nc, m, sem, ada)
        end()
        for l in range(2):
            x, h = m.region[l], m.region[1 - l]
            mm = moe_memory(m, a, keep_sem, l, m.region_at[l])

            def first_loads(sp):
                if l == 0:
                    recurrent_pre.load_x(sp, 0)
                    recurrent_pre.load_g(sp, 0)
                else:
                    attn_pre[1].ahead(sp)

            modulated_norm(*shared, l, 0, x, h, first_loads)
            end()
            if l == 0:
                recurrent_branch(*shared, x, h, x, x_dram, recurrent_pre, attn_pre[0].ahead)
                end()
            attention(*shared, l, x, h, x, x_dram, attn_pre[l], out_pre[l].ahead)
            end()
            out_projection(*shared, l, h, x, out_pre[l])
            end()
            modulated_norm(*shared, l, 1, h, x)
            end()
            ada = None
            if l == 0:
                put = placer(m, "ada1", m.scratch_at + 2 * 16384, m.end)
                slots = [put(f"w{i}", [P, KB // 2, BANK]) for i in range(2)]
                put = placer(m, "ada1s", mm.spare_at, m.end)
                slots += [put(f"w{i}", [P, KB // 2, BANK]) for i in range(2)]
                rows = [put(f"row{i}", [2, BANK]) for i in range(2)]
                ada = adaln(m, a, sem, 1, slots, rows, (6, 7), 5 * BANK)
            routing(*shared, l, x, mm, drams[l], ada)
            end()
            experts(*shared, l, h, mm, drams[l])
            end()
            add_experts(*shared, l, h, m.region_at[l], drams[l])
            end()


_OUTS = [("y_prompt", (1, CTX, D)), ("y_sample", (1, LAT, D)), ("new_l0_k", (1, CTX, 2, HD)), ("new_l0_v", (1, CTX, 2, HD)),
         ("new_l0_fwd", (1, LRU)), ("new_l0_bwd", (1, LRU)), ("new_l1_k", (1, CTX, 2, 8, HD)),
         ("new_l1_v", (1, CTX, 8, 2 * HD))]


def rope_tables():
    f32 = np.float32
    inv = (f32(10000.0) ** (-np.arange(16, dtype=f32) / f32(16))).astype(f32)
    t = np.arange(LAT)
    ang = np.stack([(t // 64).astype(f32)[:, None] * inv, (t % 64).astype(f32)[:, None] * inv], axis=1).astype(f32)
    cos, sin = np.cos(ang), np.sin(ang)
    return (np.stack([cos, cos], axis=2).reshape(LAT, HD).astype(f32),
            np.stack([sin, -sin], axis=2).reshape(LAT, HD).astype(f32))


def launch_args(nc, inputs):
    arrays, args = {}, {}
    cos, sin = rope_tables()
    for name, v in {**inputs, "rope_cos": cos, "rope_sin": sin}.items():
        v = np.ascontiguousarray(v)
        arrays[f"in_{name}"] = v
        args[name] = nc.dram_tensor(f"in_{name}", v.shape, mybir.dt.from_np(v.dtype), kind="ExternalInput").ap()
    for name, shape in _OUTS:
        args[name] = nc.dram_tensor(f"out_{name}", shape, F32, kind="ExternalOutput").ap()
    return arrays, args


def kernel(**inputs):
    import concourse.bacc as _bacc
    from concourse.bass_utils import run_bass_kernel_spmd as _run

    nc = _bacc.Bacc("TRN2", target_bir_lowering=False, num_devices=1)
    arrays, args = launch_args(nc, inputs)
    build(nc, args)
    r = _run(nc, [arrays], core_ids=[0])
    return tuple(r.results[0][f"out_{name}"] for name, _ in _OUTS)
```
